# Optimizing a Trainium2 kernel written in Bass

```python
import math
import jax, jax.numpy as jnp
from jax import lax
import numpy as np

D_MODEL = 1024
BATCH = 1
SEQ = 256
DEPTH = 2

CHUNK = 64
Q_BLOCK = 128
HEAD_DIM = 64
FOX_HEADS = 8
SB_HEADS = 8
FOX_WIDTH = FOX_HEADS * HEAD_DIM
SB_WIDTH = SB_HEADS * HEAD_DIM
BRANCH_WIDTH = FOX_WIDTH
N_BRANCHES = 2
IN_WIDTH = 3 * FOX_WIDTH + FOX_HEADS + 3 * SB_WIDTH + N_BRANCHES * D_MODEL
PEER_HEADS = 8
PEER_DK = 128
N_KEYS = 128
N_EXPERTS = N_KEYS * N_KEYS
PEER_TOPK = 16
PEER_BLOCK = 128
EPS = 1e-6

kernel_name = "hybrid_fox_stickbreak_peer_adaln"

def rmsnorm(x, gain):
    x32 = x.astype(jnp.float32)
    y = x32 * lax.rsqrt(jnp.mean(x32 * x32, axis=-1, keepdims=True) + EPS)
    return y.astype(x.dtype) * gain

def modulate(h, shift, scale):
    return h * (1.0 + scale[:, None, :]) + shift[:, None, :]

def split_heads(t, n_heads):
    b, s, _ = t.shape
    return t.reshape(b, s, n_heads, HEAD_DIM).transpose(0, 2, 1, 3)

def merge_heads(t):
    b, h, s, d = t.shape
    return t.transpose(0, 2, 1, 3).reshape(b, s, h * d)

def forgetting_attention(q, k, v, log_f):
    seq = q.shape[2]
    scale = 1.0 / math.sqrt(HEAD_DIM)
    cum_f = lax.cumsum(log_f, axis=2)
    outs = []
    for i in range(seq // Q_BLOCK):
        lo, hi = i * Q_BLOCK, (i + 1) * Q_BLOCK
        qb = q[:, :, lo:hi]
        kp = k[:, :, :hi]
        vp = v[:, :, :hi]
        logits = (jnp.einsum('bhqd,bhkd->bhqk', qb, kp) * scale
                  + cum_f[:, :, lo:hi, None] - cum_f[:, :, None, :hi])
        mask = (lo + jnp.arange(Q_BLOCK))[:, None] >= jnp.arange(hi)[None, :]
        p = jax.nn.softmax(jnp.where(mask, logits, -jnp.inf), axis=-1)
        outs.append(jnp.einsum('bhqk,bhkd->bhqd', p, vp))
    return jnp.concatenate(outs, axis=2)

def stick_breaking_attention(q, k, v):
    seq = q.shape[2]
    scale = 1.0 / math.sqrt(HEAD_DIM)
    outs = []
    for i in range(seq // Q_BLOCK):
        lo, hi = i * Q_BLOCK, (i + 1) * Q_BLOCK
        qb = q[:, :, lo:hi]
        kp = k[:, :, :hi]
        vp = v[:, :, :hi]
        z = jnp.einsum('bhqd,bhkd->bhqk', qb, kp) * scale
        mask = (lo + jnp.arange(Q_BLOCK))[:, None] > jnp.arange(hi)[None, :]
        log_one_minus = jnp.where(mask, jax.nn.log_sigmoid(-z), 0.0)
        suffix = lax.cumsum(log_one_minus, axis=3, reverse=True) - log_one_minus
        weights = jnp.where(mask, jnp.exp(jax.nn.log_sigmoid(z) + suffix), 0.0)
        outs.append(jnp.einsum('bhqk,bhkd->bhqd', weights, vp))
    return jnp.concatenate(outs, axis=2)

def qk_rmsnorm(t, gain):
    t = t * lax.rsqrt(jnp.mean(t * t, axis=-1, keepdims=True) + EPS)
    return t * gain.astype(jnp.float32)

def mixing_sublayer(h, w_in, fox_bf, fox_q_gain, fox_k_gain, w_branch, w_out):
    b, s, _ = h.shape
    proj = h @ w_in
    sizes = [FOX_WIDTH] * 3 + [FOX_HEADS] + [SB_WIDTH] * 3 + [N_BRANCHES * D_MODEL]
    points, acc = [], 0
    for sz in sizes[:-1]:
        acc += sz
        points.append(acc)
    qa, ka, va, fa, qb, kb, vb, gates = jnp.split(proj, points, axis=-1)

    f32 = jnp.float32
    qa = qk_rmsnorm(split_heads(qa, FOX_HEADS).astype(f32), fox_q_gain)
    ka = qk_rmsnorm(split_heads(ka, FOX_HEADS).astype(f32), fox_k_gain)
    va = split_heads(va, FOX_HEADS).astype(f32)
    log_f = jax.nn.log_sigmoid((fa + fox_bf).astype(f32)).transpose(0, 2, 1)
    y_fox = merge_heads(forgetting_attention(qa, ka, va, log_f)).astype(h.dtype)

    qb = split_heads(qb, SB_HEADS).astype(f32)
    kb = split_heads(kb, SB_HEADS).astype(f32)
    vb = split_heads(vb, SB_HEADS).astype(f32)
    y_sb = merge_heads(stick_breaking_attention(qb, kb, vb)).astype(h.dtype)

    branches = jnp.stack([y_fox, y_sb], axis=2)
    branches = jnp.einsum('bsgc,gcd->bsgd', branches, w_branch)
    gate = jax.nn.sigmoid(gates.reshape(b, s, N_BRANCHES, D_MODEL))
    merged = jnp.sum(gate * branches, axis=2)
    return merged @ w_out

def peer_sublayer(h, peer_wq, peer_k1, peer_k2, peer_u, peer_v):
    b, s, d = h.shape
    q = (h @ peer_wq).reshape(b, s, PEER_HEADS, PEER_DK).astype(jnp.float32)
    half = PEER_DK // 2
    s1 = jnp.einsum('bshd,hnd->bshn', q[..., :half], peer_k1.astype(jnp.float32))
    s2 = jnp.einsum('bshd,hnd->bshn', q[..., half:], peer_k2.astype(jnp.float32))
    v1, i1 = lax.top_k(s1, PEER_TOPK)
    v2, i2 = lax.top_k(s2, PEER_TOPK)
    cand = (v1[..., :, None] + v2[..., None, :]).reshape(b, s, PEER_HEADS, PEER_TOPK * PEER_TOPK)
    top_s, j = lax.top_k(cand, PEER_TOPK)
    e1 = jnp.take_along_axis(i1, j // PEER_TOPK, axis=-1)
    e2 = jnp.take_along_axis(i2, j % PEER_TOPK, axis=-1)
    idx = e1 * N_KEYS + e2
    g = jax.nn.softmax(top_s, axis=-1)

    n_blocks = (b * s) // PEER_BLOCK
    xf = h.reshape(n_blocks, PEER_BLOCK, d)
    idx_b = idx.reshape(n_blocks, PEER_BLOCK, PEER_HEADS, PEER_TOPK)
    g_b = g.reshape(n_blocks, PEER_BLOCK, PEER_HEADS, PEER_TOPK)

    def expert_block(args):
        xb, ib, gb = args
        u = jnp.take(peer_u, ib, axis=0)
        act = jax.nn.gelu(jnp.einsum('thkd,td->thk', u, xb), approximate=False)
        v = jnp.take(peer_v, ib, axis=0)
        return jnp.einsum('thk,thkd->td', (gb * act).astype(v.dtype), v)

    y = lax.map(expert_block, (xf, idx_b, g_b))
    return y.reshape(b, s, d)

def setup_inputs(seed: int = 0) -> dict:
    key = jax.random.key(seed)
    ks = jax.random.split(key, 18)
    D = D_MODEL

    def nrm(k, shape, s):
        return jax.random.normal(k, shape, jnp.float32) * s

    return {
        "x": nrm(ks[0], (BATCH, SEQ, D), 1.0),
        "c": nrm(ks[1], (BATCH, D), 1.0),
        "ada_w": nrm(ks[2], (DEPTH, D, 6 * D), 0.5 * D ** -0.5),
        "ada_b": nrm(ks[3], (DEPTH, 6 * D), 0.02),
        "attn_norm": 1.0 + nrm(ks[4], (DEPTH, D), 0.02),
        "ffn_norm": 1.0 + nrm(ks[5], (DEPTH, D), 0.02),
        "w_in": nrm(ks[6], (DEPTH, D, IN_WIDTH), D ** -0.5),
        "fox_bf": jnp.linspace(1.0, 5.0, FOX_HEADS, dtype=jnp.float32)[None, :]
                  + nrm(ks[7], (DEPTH, FOX_HEADS), 0.1),
        "fox_q_gain": 1.0 + nrm(ks[8], (DEPTH, HEAD_DIM), 0.02),
        "fox_k_gain": 1.0 + nrm(ks[9], (DEPTH, HEAD_DIM), 0.02),
        "w_branch": nrm(ks[10], (DEPTH, N_BRANCHES, BRANCH_WIDTH, D), BRANCH_WIDTH ** -0.5),
        "w_out": nrm(ks[11], (DEPTH, D, D), D ** -0.5),
        "peer_wq": nrm(ks[12], (DEPTH, D, PEER_HEADS * PEER_DK), D ** -0.5),
        "peer_k1": nrm(ks[13], (DEPTH, PEER_HEADS, N_KEYS, PEER_DK // 2), (PEER_DK // 2) ** -0.5),
        "peer_k2": nrm(ks[14], (DEPTH, PEER_HEADS, N_KEYS, PEER_DK // 2), (PEER_DK // 2) ** -0.5),
        "peer_u": nrm(ks[15], (DEPTH, N_EXPERTS, D), D ** -0.5),
        "peer_v": nrm(ks[16], (DEPTH, N_EXPERTS, D), 1.0),
    }

def reference(x, c, ada_w, ada_b, attn_norm, ffn_norm, w_in, fox_bf, fox_q_gain,
              fox_k_gain, w_branch, w_out, peer_wq, peer_k1, peer_k2, peer_u, peer_v):
    for l in range(DEPTH):
        mod = jax.nn.silu(c) @ ada_w[l] + ada_b[l]
        sh1, sc1, g1, sh2, sc2, g2 = jnp.split(mod, 6, axis=-1)
        h = modulate(rmsnorm(x, attn_norm[l]), sh1, sc1)
        x = x + g1[:, None, :] * mixing_sublayer(
            h, w_in[l], fox_bf[l], fox_q_gain[l], fox_k_gain[l], w_branch[l], w_out[l])
        h = modulate(rmsnorm(x, ffn_norm[l]), sh2, sc2)
        x = x + g2[:, None, :] * peer_sublayer(
            h, peer_wq[l], peer_k1[l], peer_k2[l], peer_u[l], peer_v[l])
    return x


_drawn_inputs = setup_inputs


def setup_inputs(seed=0):
    import zlib

    import numpy as np

    out = dict(_drawn_inputs(seed))
    spreads = {}
    factors = {'attn_norm': 3.087, 'fox_q_gain': 5.63, 'fox_k_gain': 5.832}
    for name, (base, spread) in spreads.items():
        noise = np.random.default_rng([zlib.crc32(name.encode()), seed]).standard_normal(out[name].shape)
        drawn = base * np.exp(spread * noise) if base else spread * noise
        out[name] = __import__('jax').numpy.asarray(drawn.astype(out[name].dtype))
    for name, factor in factors.items():
        out[name] = (out[name] * factor).astype(out[name].dtype)
    return out
```

```python
from contextlib import ExitStack

import concourse.bass as bass
from concourse import mybir

ALU = mybir.AluOpType
ACT = mybir.ActivationFunctionType
AX = mybir.AxisListType
F32 = mybir.dt.float32
F32R = mybir.dt.float32r
U32 = mybir.dt.uint32

P = 128
D = 1024
T = 256
L = 2
H = 8
HD = 64
KEYS = 128
TOPK = 16
PAIRS = H * TOPK
EPS = 1e-6
NEG = -1e30
LOWEST = -3e38

TB = T // P
K = D // P
COLS = 512
IN_WIDTH = 5128
FA = 3 * H * HD
N_ADA = 6 * D // COLS
N_PROJ = (IN_WIDTH - H) // COLS
N_BRANCH = N_OUT = N_WQ = D // COLS
N_WEIGHTS = N_PROJ + N_BRANCH + N_OUT + N_WQ
N_SHIFT = 2 * D // COLS
N_LATER = N_ADA - N_SHIFT
AT_BRANCH = N_PROJ
AT_OUT = AT_BRANCH + N_BRANCH
AT_WQ = AT_OUT + N_OUT
SLOTS = 3


def ada_place(n):
    return [(0, 0), (1, 0), (2, 0), (0, 1)][n] if n < 4 else (2, n - 3)


def weight_place(n):
    return 1 - n % 2, 1 + n % 2 + n // 2


SLOT_USES = [N_WEIGHTS // 2 + 2, N_WEIGHTS // 2 + 1, N_ADA - 3]
BLOCKS = KEYS
EARLY = 64
MIDDLE = 32
LATE_AT = EARLY + MIDDLE
GROUP = 4
N_GROUPS = T // GROUP
CAUSAL = 3 * P
AUG = HD + 2

PAR = 6 * K + 2 * K
ROWC = 2 * HD + H


class Signal:

    def __init__(self, ctx, nc, name, per_layer=0):
        self.sem = ctx.enter_context(nc.semaphore(name))
        self.per_layer = per_layer

    def by(self, layer, count):
        return layer * self.per_layer + count


def hybrid_fox_stickbreak_peer(nc, x, c, ada_w, ada_b, attn_norm, ffn_norm, w_in, fox_bf, fox_q_gain,
                               fox_k_gain, w_branch, w_out, peer_wq, peer_k1, peer_k2, peer_u, peer_v, out):
    ctx = ExitStack()
    with ctx:
        def sb(name, shape, dt=F32):
            return ctx.enter_context(nc.sbuf_tensor(name, shape, dt))

        x_sb = sb("x_sb", [P, TB, D])
        ident = sb("ident", [P, P])
        ones = sb("ones", [P, P])
        neg_ones = sb("neg_ones", [P, P])
        cumsum_tri = sb("cumsum_tri", [P, P])
        neg_suffix_tri = sb("neg_suffix_tri", [P, P])
        fox_mask = sb("fox_mask", [P, P])
        sb_mask = sb("sb_mask", [P, P])
        sb_keep = sb("sb_keep", [P, P])
        iota = sb("iota", [P, P])
        par_t = sb("par_t", [P, L * PAR])
        c_t = sb("c_t", [P, K])
        rows_bc = sb("rows_bc", [P, L * ROWC])
        mod = sb("mod", [P, 6 * K])
        gain = sb("gain", [P, 2, K])
        stat = sb("stat", [P, 2, TB])
        small = sb("small", [P, 96])
        eps = sb("eps", [P, 1])
        h_hi = sb("h_hi", [P, K, T], F32R)
        h_lo = sb("h_lo", [P, K, T], F32R)
        rows_in = sb("rows_in", [P, 4, D])
        rows_hi = sb("rows_hi", [P, 2, D], F32R)
        rows_lo = sb("rows_lo", [P, 2, D], F32R)
        ada_sum = sb("ada_sum", [P, 2, COLS])
        act = sb("act", [P, 2, T])
        w_hi = sb("w_hi", [P, 2, T], F32R)
        w_lo = sb("w_lo", [P, 2, T], F32R)
        route_t = sb("route_t", [P, 3, T])
        hot2 = rows_in[:, 2, :].rearrange("p (t n) -> p t n", n=P)
        hot1 = rows_in[:, 3, :].rearrange("p (t n) -> p t n", n=P)
        par_rows = rows_in[:, 0, 0:P]
        c_rows = rows_in[0:K, 0, P:2 * P]
        row_consts = rows_in[0:1, 0, 2 * P:2 * P + L * ROWC]

        arena = sb("arena", [P, T * KEYS])
        weight = arena[:, :].rearrange("p (e t) -> p e t", t=T)
        cursor = [0]

        def part(words):
            cursor[0] += words
            return arena[:, cursor[0] - words:cursor[0]]

        h_t = part(K * T).rearrange("p (k t) -> p k t", k=K)
        w_slot = part(2 * K * COLS).rearrange("p (s k n) -> p s k n", s=2, k=K)
        slots = [w_slot[:, 0], w_slot[:, 1], rows_in[:, :, :].rearrange("p a (k n) -> p (a k) n", n=COLS)]
        qk_words = part(H * COLS + H // 2 * COLS)
        y_words = part(2 * 4 * T)
        y_t = y_words.rearrange("p (c t) -> p c t", t=T)
        aug_words = part(2 * TB * H * AUG)
        tmp = part(T * KEYS - TB * N_PROJ * COLS - cursor[0])
        proj_words = part(TB * N_PROJ * COLS)
        proj = proj_words.rearrange("p (b n) -> p b n", b=TB)
        fox_qk = qk_words[:, 0:H * COLS].rearrange("p (h n) -> p h n", h=H)
        sb_qk = qk_words[:, H * COLS:].rearrange("p (h n) -> p h n", h=H // 2)
        x_norm = qk_words[:, 0:TB * D].rearrange("p (b n) -> p b n", b=TB)
        junk = qk_words[:, 4096:4096 + D]
        sq_junk = qk_words[:, 4096 + D:4096 + D + COLS].rearrange("p (h n) -> p h n", h=H)
        merged = qk_words[:, 0:TB * D].rearrange("p (b n) -> p b n", b=TB)
        pq_t = qk_words[:, TB * D:TB * D + H * T].rearrange("p (h t) -> p h t", h=H)
        gate_row = y_words[:, 0:D]
        aug = aug_words.rearrange("p (w b h e) -> p w b h e", w=2, b=TB, h=H)
        diag = aug_words[:, 0:D].rearrange("p (k n) -> p k n", k=K)
        keys = aug_words[:, D:D + H * P].rearrange("p (h n) -> p h n", h=H)
        probs = tmp[:, 0:2 * CAUSAL].rearrange("p (s n) -> p s n", s=2)
        probs_t = tmp[:, 2 * CAUSAL:4 * CAUSAL].rearrange("p (s n) -> p s n", s=2)
        keys_t = tmp[:, 0:H * P].rearrange("p (h n) -> p h n", h=H)
        forget_w = tmp[:, 4 * CAUSAL:4 * CAUSAL + K * H].rearrange("p (k n) -> p k n", k=K)
        soft = proj[:, 0, 0:2 * CAUSAL].rearrange("p (s n) -> p s n", s=2)
        log_keep = proj[:, 1, 0:2 * CAUSAL].rearrange("p (s n) -> p s n", s=2)
        gates = proj[:, :, 6 * COLS:]
        score = proj_words[:, 0:TB * 2 * D].rearrange("p (b r n) -> p b r n", b=TB, n=KEYS)
        cand_words = proj_words[:, 4 * D:6 * D]
        cand = cand_words.rearrange("p (h a b) -> p h a b", h=H, a=TOPK)
        onehot = cand_words.rearrange("p (m a) -> p m a", a=TOPK)
        routing = proj_words[:, 6 * D:]
        taken = [0]

        def route_part(words):
            taken[0] += words
            return routing[:, taken[0] - words:taken[0]]

        top1 = route_part(256).rearrange("p (r k) -> p r k", k=TOPK)
        top1_at = route_part(256).bitcast(U32).rearrange("p (r k) -> p r k", k=TOPK)
        top1_f = route_part(256).rearrange("p (r k) -> p r k", k=TOPK)
        top2 = route_part(TB * PAIRS).rearrange("p (b h k) -> p b h k", b=TB, k=TOPK)
        top2_at = route_part(TB * PAIRS).bitcast(U32).rearrange("p (b m) -> p b m", b=TB)
        digit = route_part(PAIRS).bitcast(U32)
        digit_f = route_part(PAIRS)
        routed = route_part(TB * 3 * PAIRS).rearrange("p (b w m) -> p b w m", b=TB, w=3)

        bank = [ctx.enter_context(nc.psum_tensor(f"bank{n}", [P, COLS], F32)) for n in range(8)]
        y_bank = bank[0:4]
        ut_bank = bank[4:6]
        act_bank = bank[6:8]
        gate_bank = bank[0:4]

        def score_bank(b, m):
            return bank[(4 if b == 0 else 0) + m][:, :].rearrange("p (r n) -> p r n", n=KEYS)

        def signal(name, per_layer=0):
            return Signal(ctx, nc, name, per_layer)

        inputs_in = signal("inputs_in")
        masks_made = signal("masks_made")
        setup_transposed = signal("setup_transposed")
        setup_done = signal("setup_done")
        arena_free = signal("arena_free", 1)
        slots_free = signal("slots_free", 1)
        slot_in = [signal(f"slot_in{s}", 16 * SLOT_USES[s]) for s in range(SLOTS)]
        ada_summed = signal("ada_summed", N_ADA)
        forget_w_in = signal("forget_w_in", 16)
        keys_in = signal("keys_in", 32)
        mod_summed = signal("mod_summed", N_ADA)
        mod_made = signal("mod_made", N_ADA)
        gain_made = signal("gain_made", 2)
        squares = signal("squares", 2 * TB)
        root_made = signal("root_made", 2)
        normed = signal("normed", 2 * TB)
        qk_mean = signal("qk_mean", 2 * TB)
        qk_root = signal("qk_root", 2 * TB)
        norm_transposed = signal("norm_transposed", 2 * 4)
        h_t_made = signal("h_t_made", 2 * 2 * K)
        proj_summed = signal("proj_summed", TB * N_PROJ)
        proj_kept = signal("proj_kept", TB * N_PROJ)
        forget_summed = signal("forget_summed", 1)
        forget_abs = signal("forget_abs", 1)
        forget_log = signal("forget_log", 2)
        log_f_made = signal("log_f_made", 1)
        cum_f_summed = signal("cum_f_summed", 1)
        aug_made = signal("aug_made", 1)
        qk_turned = signal("qk_turned", H + H // 2)
        qk_kept = signal("qk_kept", H + H // 2)
        fox_scored = signal("fox_scored", H)
        fox_max = signal("fox_max", H)
        fox_exp = signal("fox_exp", 2 * H)
        fox_probs = signal("fox_probs", H)
        probs_turned = signal("probs_turned", H)
        probs_kept = signal("probs_kept", H)
        sb_scored = signal("sb_scored", H)
        sb_abs = signal("sb_abs", H)
        sb_log = signal("sb_log", 2 * H)
        sb_keep_made = signal("sb_keep_made", H)
        sb_summed = signal("sb_summed", H)
        sb_weights = signal("sb_weights", H)
        y_summed = signal("y_summed", H)
        y_kept = signal("y_kept", H)
        gates_made = signal("gates_made", TB)
        branch_summed = signal("branch_summed", 4)
        merged_made = signal("merged_made", 4)
        merged_turned = signal("merged_turned", 4)
        merged_kept = signal("merged_kept", 4)
        diag_made = signal("diag_made", 2)
        row_summed = signal("row_summed", 2 * 2)
        row_kept = signal("row_kept", 2 * 2)
        out_summed = signal("out_summed", 4)
        x_mixed = signal("x_mixed", 4)
        h_split = signal("h_split", 2)
        pq_summed = signal("pq_summed", H)
        pq_kept = signal("pq_kept", H)
        keys_turned = signal("keys_turned", 2)
        keys_kept = signal("keys_kept", 2)
        scored = signal("scored", 4 * TB)
        scores_kept = signal("scores_kept", 3 * TB)
        last_scores_kept = signal("last_scores_kept", TB)
        soft_sub = signal("soft_sub", TB)
        soft_exp = signal("soft_exp", 1)
        route_made = signal("route_made", 1)
        route_turned = signal("route_turned", TB)
        route_kept = signal("route_kept", TB)
        hot_made = signal("hot_made", N_GROUPS)
        gates_summed = signal("gates_summed", N_GROUPS)
        gates_kept = signal("gates_kept", N_GROUPS)
        gates_used = signal("gates_used", N_GROUPS)
        ones_laid = signal("ones_laid", 2)
        u_landed = [signal(f"u_landed{s}", 16 * BLOCKS // 2) for s in range(2)]
        v_landed = [signal(f"v_landed{s}", 16 * BLOCKS // 4) for s in range(4)]
        ut_turned = signal("ut_turned", 2 * BLOCKS)
        ut_hi_made = signal("ut_hi_made", 2 * BLOCKS)
        ut_lo_made = signal("ut_lo_made", 2 * BLOCKS)
        act_summed = signal("act_summed", BLOCKS)
        act_made = signal("act_made", BLOCKS)
        weight_made = signal("weight_made", BLOCKS - EARLY)
        w_hi_made = signal("w_hi_made", BLOCKS)
        w_split = signal("w_split", BLOCKS)
        v_hi_made = signal("v_hi_made", BLOCKS)
        v_split = signal("v_split", BLOCKS)
        y_added = signal("y_added", BLOCKS)
        x_done = signal("x_done", 4)
        stored = signal("stored")
        dve_step = signal("dve_step")

        BETWEEN = 1.6
        MASKS = 16

        block = ctx.enter_context(nc.Block())

        @block.sync
        def _(sp):
            sp.dma_start(x_sb[:, :, :], x.rearrange("o (b p) d -> p (o b) d", p=P)).then_inc(inputs_in.sem, 16)
            sp.dma_start(c_rows, c.rearrange("o (k p) -> (o k) p", p=P)).then_inc(inputs_in.sem, 16)
            for l in range(L):
                at = l * PAR
                for rows, n in ((ada_b, 6 * K), (attn_norm, K), (ffn_norm, K)):
                    sp.dma_start(par_rows[at:at + n, :], rows[l, :].rearrange("(k p) -> k p", p=P))\
                        .then_inc(inputs_in.sem, 16)
                    at += n
                at = l * ROWC
                for rows, n in ((fox_q_gain, HD), (fox_k_gain, HD), (fox_bf, H)):
                    sp.dma_start(row_consts[:, at:at + n], rows[l:l + 1, :]).then_inc(inputs_in.sem, 16)
                    at += n
            with sp.Fori(0, L) as l:
                sp.wait_ge(slots_free.sem, slots_free.by(l, 1))

                def products_made(n):
                    for summed, each, first, after in ((proj_summed, TB, 0, AT_BRANCH),
                                                       (branch_summed, TB, AT_BRANCH, AT_OUT),
                                                       (out_summed, TB, AT_OUT, AT_WQ),
                                                       (pq_summed, H // N_WQ, AT_WQ, N_WEIGHTS)):
                        if first <= n < after:
                            sp.wait_ge(summed.sem, summed.by(l, each * (n - first + 1)))

                def slot_free(n):
                    if n < 2:
                        before = (1, 3)[n]
                        sp.wait_ge(ada_summed.sem, ada_summed.by(l, before + 1))
                    else:
                        products_made(n - 2)

                def load(slot, weight, col):
                    src = weight[bass.ds(l * D, D), col:col + COLS].rearrange("(k p) n -> p k n", p=P)
                    sp.dma_start(slots[slot], src).then_inc(slot_in[slot].sem, 16)

                def weight_chunk(n, weight, col, wait=True):
                    if wait:
                        slot_free(n)
                    load(weight_place(n)[0], weight, col)

                ada_rows = ada_w.rearrange("l d n -> (l d) n")
                in_rows = w_in.rearrange("l d n -> (l d) n")

                def ada_chunk(n):
                    if n == 2:
                        sp.wait_ge(v_split.sem, v_split.by(l, 0))
                    elif n > 2:
                        before = 0 if n == 3 else 2 if n == 4 else n - 1
                        sp.wait_ge(ada_summed.sem, ada_summed.by(l, before + 1))
                    load(ada_place(n)[0], ada_rows, n * COLS)

                for n in range(N_SHIFT):
                    ada_chunk(n)
                slot_free(0)
                sp.dma_start(forget_w, in_rows[bass.ds(l * D, D), FA:FA + H]
                             .rearrange("(k p) n -> p k n", p=P)).then_inc(forget_w_in.sem, 16)
                for n in range(N_PROJ):
                    weight_chunk(n, in_rows, n * COLS + (H if n * COLS >= FA else 0), wait=n > 0)
                    if 1 <= n <= N_LATER:
                        ada_chunk(N_SHIFT + n - 1)
                for n in range(N_BRANCH):
                    weight_chunk(AT_BRANCH + n, w_branch.rearrange("l g c n -> (l g c) n"), n * COLS)
                for n in range(N_OUT):
                    weight_chunk(AT_OUT + n, w_out.rearrange("l d n -> (l d) n"), n * COLS)
                for n, k_part in enumerate((peer_k1, peer_k2)):
                    sp.dma_start(keys[:, :, n * HD:(n + 1) * HD],
                                 k_part.rearrange("l h n d -> (l h) n d")[bass.ds(l * H, H)]
                                 .rearrange("h n d -> n h d")).then_inc(keys_in.sem, 16)
                for n in range(N_WQ):
                    weight_chunk(AT_WQ + n, peer_wq.rearrange("l d n -> (l d) n"), n * COLS)

                u_rows = peer_u.rearrange("l e d -> (l e) d")
                v_rows = peer_v.rearrange("l e d -> (l e) d")

                def expert_rows(landed, at, rows, n):
                    row = (l * BLOCKS + n) * KEYS
                    sp.dma_start(rows_in[:, at], rows[bass.ds(row, KEYS), :]).then_inc(landed.sem, 16)

                sp.wait_ge(ada_summed.sem, ada_summed.by(l, N_ADA))
                for s in range(2):
                    expert_rows(u_landed[s], s, u_rows, s)
                with sp.Fori(1, BLOCKS // 2) as i:
                    for s in range(2):
                        n = 2 * i + s
                        sp.wait_ge(ut_turned.sem, ut_turned.by(l, 2 * (n - 1)))
                        expert_rows(u_landed[s], s, u_rows, n)
                for n in range(4):
                    if n >= 2:
                        sp.wait_ge(ut_turned.sem, ut_turned.by(l, 2 * (BLOCKS + n - 3)))
                    expert_rows(v_landed[n], (n + 2) % 4, v_rows, n)
                with sp.Fori(1, BLOCKS // 4) as i:
                    for s in range(4):
                        n = 4 * i + s
                        sp.wait_ge(v_split.sem, v_split.by(l, n - 3))
                        expert_rows(v_landed[s], (s + 2) % 4, v_rows, n)
            sp.wait_ge(x_done.sem, L * 4)
            sp.dma_start(out.rearrange("o (b p) d -> p (o b) d", p=P), x_sb[:, :, :]).then_inc(stored.sem, 16)
            sp.wait_ge(stored.sem, 16)

        @block.gpsimd
        def _(pool):
            made = 0

            def mask(tile, value, fill, op, step, channel):
                nonlocal made
                nc.gpsimd.memset(tile[:, :], value).then_inc(masks_made.sem, 1)
                pool.wait_ge(masks_made.sem, made + 1)
                nc.gpsimd.affine_select(out=tile[:, :], in_=tile[:, :], compare_op=op, fill=fill, base=0,
                                        pattern=[[step, P]], channel_multiplier=channel)\
                    .then_inc(masks_made.sem, 1)
                made += 2

            mask(ident, 0.0, 1.0, ALU.not_equal, -1, 1)
            mask(cumsum_tri, 1.0, 0.0, ALU.is_ge, 1, -1)
            mask(neg_suffix_tri, -1.0, 0.0, ALU.is_ge, -1, 1)
            mask(fox_mask, NEG, 0.0, ALU.is_gt, 1, -1)
            mask(sb_mask, NEG, 0.0, ALU.is_ge, -1, 1)
            mask(sb_keep, 1.0, 0.0, ALU.is_gt, 1, -1)
            nc.gpsimd.memset(ones[:, :], 1.0).then_inc(masks_made.sem, 1)
            nc.gpsimd.memset(neg_ones[:, :], -1.0).then_inc(masks_made.sem, 1)
            nc.gpsimd.memset(eps[:, :], EPS).then_inc(masks_made.sem, 1)
            nc.gpsimd.iota(iota[:, :], [[1, P]], base=0, channel_multiplier=0,
                           allow_small_or_imprecise_dtypes=True).then_inc(masks_made.sem, 1)
            assert made + 4 == MASKS

            behind_proj = (T * KEYS - TB * N_PROJ * COLS) // T

            def lay_ones(first, after):
                to = arena[:, first * T:after * T]
                one = ones[:, 0:1].to_broadcast([P, (after - first) * T])
                nc.gpsimd.tensor_tensor(to, one, one, ALU.mult).then_inc(ones_laid.sem, 1)

            pool.wait_ge(masks_made.sem, MASKS)
            with pool.Fori(0, L) as l:
                pool.wait_ge(scored.sem, scored.by(l, 4 * TB))
                lay_ones(EARLY, behind_proj)
                pool.wait_ge(soft_sub.sem, soft_sub.by(l, 1))
                lay_ones(behind_proj, LATE_AT)

        @block.scalar
        def _(sc):
            sc.wait_ge(setup_transposed.sem, 3)
            nc.scalar.activation(par_t[:, :], bank[0][:, 0:P], ACT.Copy).then_inc(setup_done.sem, 1)
            nc.scalar.activation(c_t[:, :], bank[1][:, 0:K], ACT.Silu).then_inc(setup_done.sem, 1)
            nc.scalar.activation(rows_bc[:, :], bank[2][:, 0:L * ROWC], ACT.Copy).then_inc(setup_done.sem, 1)

            with sc.Fori(0, L) as l:
                def norm(which):
                    for b in range(TB):
                        if which == 0:
                            sc.wait_ge(arena_free.sem, arena_free.by(l, 1))
                        else:
                            sc.wait_ge(x_mixed.sem, x_mixed.by(l, 4))
                        if b:
                            sc.wait_ge(squares.sem, squares.by(l, which * TB + b))
                        nc.scalar.activation(junk, x_sb[:, b], ACT.Square, scale=D ** -0.5,
                                             accum_out=stat[:, 0, b:b + 1])\
                            .then_inc(squares.sem, 1)
                    sc.wait_ge(squares.sem, squares.by(l, TB * (which + 1)))
                    nc.scalar.activation(stat[:, 1], stat[:, 0], ACT.Sqrt, bias=eps[:, :]).then_inc(root_made.sem, 1)
                    sc.wait_ge(gain_made.sem, gain_made.by(l, which + 1))
                    for k in range(K):
                        sc.wait_ge(norm_transposed.sem, norm_transposed.by(l, 4 * which + 1 + k // 4))
                        nc.scalar.activation(h_t[:, k, 0:P], bank[4 + k // 4][:, k % 4 * P:(k % 4 + 1) * P],
                                             ACT.Identity, scale=gain[:, which, k:k + 1],
                                             bias=mod[:, 3 * which * K + k:3 * which * K + k + 1])\
                            .then_inc(h_t_made.sem, 1)

                norm(0)

                def keep_projection(n, s):
                    for b in range(TB):
                        sc.wait_ge(proj_summed.sem, proj_summed.by(l, 2 * n + b + 1))
                        at = slice(n * COLS, (n + 1) * COLS) if isinstance(n, int) else bass.ds(n * COLS, COLS)
                        nc.scalar.activation(proj[:, b, at], bank[2 * s + b][:, :], ACT.Copy)\
                            .then_inc(proj_kept.sem, 1)

                for n in range(3):
                    keep_projection(n, n % 2)
                for n in range(2 * TB):
                    sc.wait_ge(qk_mean.sem, qk_mean.by(l, n + 1))
                    means = small[:, 64 + n * H:64 + (n + 1) * H]
                    nc.scalar.activation(means, means, ACT.Sqrt, bias=eps[:, :]).then_inc(qk_root.sem, 1)
                keep_projection(3, 1)
                sc.wait_ge(forget_abs.sem, forget_abs.by(l, 1))
                nc.scalar.activation(small[:, 16:32], small[:, 16:32], ACT.Exp, scale=-1.0)\
                    .then_inc(forget_log.sem, 1)
                sc.wait_ge(forget_log.sem, forget_log.by(l, 1))
                nc.scalar.activation(small[:, 16:32], small[:, 16:32], ACT.Ln, bias=1.0)\
                    .then_inc(forget_log.sem, 1)
                with sc.Fori(2, N_PROJ // 2) as i:
                    for s in range(2):
                        keep_projection(2 * i + s, s)

                def keep_qk(n):
                    sc.wait_ge(qk_turned.sem, qk_turned.by(l, n + 1))
                    src = bank[4 + n % 2]
                    if n < H:
                        nc.scalar.activation(fox_qk[0:AUG, n], src[0:AUG, :], ACT.Copy).then_inc(qk_kept.sem, 1)
                    else:
                        nc.scalar.activation(sb_qk[:, n - H, 0:T], src[:, 0:T], ACT.Copy, scale=HD ** -0.5)
                        nc.scalar.activation(sb_qk[:, n - H, T:2 * T], src[:, T:2 * T], ACT.Copy)\
                            .then_inc(qk_kept.sem, 1)

                def fox_exps(h):
                    sc.wait_ge(fox_max.sem, fox_max.by(l, h + 1))
                    if h >= 2:
                        sc.wait_ge(probs_turned.sem, probs_turned.by(l, h - 1))
                    for b, (at, n) in enumerate(((0, P), (P, 2 * P))):
                        nc.scalar.activation(probs[:, h % 2, at:at + n], bank[h % 2][:, at:at + n], ACT.Exp,
                                             bias=small[:, 40 + 2 * (h % 2) + b:41 + 2 * (h % 2) + b],
                                             accum_out=small[:, 48 + 2 * (h % 2) + b:49 + 2 * (h % 2) + b])\
                            .then_inc(fox_exp.sem, 1)

                def keep_probs(h):
                    sc.wait_ge(probs_turned.sem, probs_turned.by(l, h + 1))
                    if h >= 2 and h % 2 == 0:
                        sc.wait_ge(y_summed.sem, y_summed.by(l, h // 2))
                    nc.scalar.activation(probs_t[:, h % 2], bank[2 + h % 2][:, 0:CAUSAL], ACT.Copy)\
                        .then_inc(probs_kept.sem, 1)

                def keep_y(n):
                    sc.wait_ge(y_summed.sem, y_summed.by(l, n + 1))
                    nc.scalar.activation(y_t[:, n], bank[6 + n % 2][:, 0:T], ACT.Copy).then_inc(y_kept.sem, 1)

                keep_qk(0)
                keep_qk(1)
                for h in range(H + 1):
                    if h < H:
                        fox_exps(h)
                    if h + 2 < H:
                        keep_qk(h + 2)
                    if h >= 1:
                        keep_probs(h - 1)
                        if h % 2 == 0:
                            keep_y(h // 2 - 1)
                for n in range(H, H + H // 2):
                    keep_qk(n)

                def softplus_tail(h):
                    s = h % 2
                    sc.wait_ge(sb_scored.sem, sb_scored.by(l, h + 1))
                    if h >= 2:
                        sc.wait_ge(sb_keep_made.sem, sb_keep_made.by(l, h - 1))
                    nc.scalar.activation(soft[:, s], bank[s][:, 0:CAUSAL], ACT.Abs).then_inc(sb_abs.sem, 1)
                    sc.wait_ge(sb_abs.sem, sb_abs.by(l, h + 1))
                    nc.scalar.activation(soft[:, s], soft[:, s], ACT.Exp, scale=-1.0).then_inc(sb_log.sem, 1)
                    sc.wait_ge(sb_log.sem, sb_log.by(l, 2 * h + 1))
                    nc.scalar.activation(soft[:, s], soft[:, s], ACT.Ln, bias=1.0).then_inc(sb_log.sem, 1)

                def sb_exp(h):
                    sc.wait_ge(sb_summed.sem, sb_summed.by(l, h + 1))
                    if h % 2 == 0:
                        sc.wait_ge(y_summed.sem, y_summed.by(l, H // 2 + h // 2))
                    nc.scalar.activation(probs_t[:, h % 2], bank[2 + h % 2][:, 0:CAUSAL], ACT.Exp)\
                        .then_inc(sb_weights.sem, 1)

                for h in range(H + 1):
                    if h < H:
                        softplus_tail(h)
                    if h >= 1:
                        sb_exp(h - 1)
                        if h % 2 == 0:
                            keep_y(H // 2 + h // 2 - 1)
                for b in range(TB):
                    nc.scalar.activation(gates[:, b], gates[:, b], ACT.Sigmoid).then_inc(gates_made.sem, 1)
                for n in range(4):
                    sc.wait_ge(merged_turned.sem, merged_turned.by(l, n + 1))
                    dst = h_t[:, 4 * (n % 2):4 * (n % 2) + 4, n // 2 * P:(n // 2 + 1) * P]
                    nc.scalar.activation(dst, bank[4 + n][:, :].rearrange("p (k t) -> p k t", k=4), ACT.Copy)\
                        .then_inc(merged_kept.sem, 1)

                def keep_row(which):
                    for n in range(2):
                        src = bank[n if which == 0 else 4 + n]
                        sc.wait_ge(row_summed.sem, row_summed.by(l, 2 * which + n + 1))
                        nc.scalar.activation(gate_row[:, n * COLS:(n + 1) * COLS], src[:, :], ACT.Copy)\
                            .then_inc(row_kept.sem, 1)

                keep_row(0)
                norm(1)
                sc.wait_ge(h_t_made.sem, h_t_made.by(l, 4 * K))
                nc.scalar.activation(h_hi[:, :, :], h_t, ACT.Copy).then_inc(h_split.sem, 1)
                for h in range(H):
                    sc.wait_ge(pq_summed.sem, pq_summed.by(l, h + 1))
                    nc.scalar.activation(pq_t[:, h], bank[h % 2][:, 0:T], ACT.Copy).then_inc(pq_kept.sem, 1)
                for n in range(2):
                    sc.wait_ge(keys_turned.sem, keys_turned.by(l, n + 1))
                    nc.scalar.activation(keys_t[:, 4 * n:4 * n + 4],
                                         bank[2 + n][:, :].rearrange("p (h n) -> p h n", n=P), ACT.Copy)\
                        .then_inc(keys_kept.sem, 1)
                for b in range(TB):
                    for n in range(3):
                        m = 2 * (n % 2) + n // 2
                        sc.wait_ge(scored.sem, scored.by(l, 4 * b + n + 1))
                        nc.scalar.activation(score[:, b, 4 * m:4 * m + 4], score_bank(b, m), ACT.Copy)\
                            .then_inc(scores_kept.sem, 1)

                def ut_high(n, s, wait=True):
                    if wait:
                        sc.wait_ge(act_summed.sem, act_summed.by(l, n - 1))
                    for half in range(2):
                        sc.wait_ge(ut_turned.sem, ut_turned.by(l, 2 * n + half + 1))
                        nc.scalar.activation(rows_hi[:, s, half * COLS:(half + 1) * COLS], ut_bank[half][:, :],
                                             ACT.Copy).then_inc(ut_hi_made.sem, 1)

                def gelu_early(n, s):
                    sc.wait_ge(act_summed.sem, act_summed.by(l, n + 1))
                    at = n if isinstance(n, int) else bass.ds(n, 1)
                    out = weight[:, at] if isinstance(n, int) else weight[:, at].squeeze(1)
                    nc.scalar.activation(out, act_bank[s][:, 0:T], ACT.Gelu).then_inc(act_made.sem, 1)

                def gelu(n, s):
                    sc.wait_ge(act_summed.sem, act_summed.by(l, n + 1))
                    if not isinstance(n, int) or n >= EARLY + 2:
                        sc.wait_ge(weight_made.sem, weight_made.by(l, n - EARLY - 1))
                    nc.scalar.activation(act[:, s], act_bank[s][:, 0:T], ACT.Gelu).then_inc(act_made.sem, 1)

                ut_high(0, 0, wait=False)
                ut_high(1, 1, wait=False)
                gelu_early(0, 0)
                ut_high(2, 0)
                gelu_early(1, 1)
                with sc.Fori(1, EARLY // 2) as i:
                    for s in range(2):
                        ut_high(2 * i + s + 1, 1 - s)
                        gelu_early(2 * i + s, s)
                sc.wait_ge(soft_sub.sem, soft_sub.by(l, TB))
                nc.scalar.activation(top2, top2, ACT.Exp).then_inc(soft_exp.sem, 1)
                for b in range(TB):
                    sc.wait_ge(route_turned.sem, route_turned.by(l, b + 1))
                    nc.scalar.activation(route_t[:, :, b * P:(b + 1) * P],
                                         bank[b][:, 0:3 * P].rearrange("p (w t) -> p w t", w=3), ACT.Copy)\
                        .then_inc(route_kept.sem, 1)
                def keep_gates(g, j):
                    sc.wait_ge(gates_summed.sem, gates_summed.by(l, g + 1))
                    of = gate_bank[j][:, :].rearrange("p (t e) -> p t e", t=GROUP)
                    at = slice(g * GROUP, (g + 1) * GROUP) if isinstance(g, int) else bass.ds(g * GROUP, GROUP)
                    nc.scalar.activation(weight[:, LATE_AT:, at].rearrange("p e t -> p t e"), of[:, :, LATE_AT:],
                                         ACT.Copy).then_inc(gates_kept.sem, 1)

                def gates_and_block(i, m):
                    for j in (2 * m, 2 * m + 1):
                        keep_gates(4 * i + j, j)
                    ut_high(EARLY + 2 * i + m + 1, 1 - m)
                    gelu(EARLY + 2 * i + m, m)

                for m in range(2):
                    gates_and_block(0, m)
                with sc.Fori(1, MIDDLE // 2) as i:
                    for m in range(2):
                        gates_and_block(i, m)
                with sc.Fori(LATE_AT // 2, BLOCKS // 2 - 1) as i:
                    for s in range(2):
                        ut_high(2 * i + s + 1, 1 - s)
                        gelu(2 * i + s, s)
                ut_high(BLOCKS - 1, 1)
                gelu(BLOCKS - 2, 0)
                gelu(BLOCKS - 1, 1)

                def v_high(n, s, i):
                    sc.wait_ge(v_landed[s].sem, v_landed[s].by(l, 16 * i + 16))
                    if not isinstance(n, int) or n >= 2:
                        sc.wait_ge(y_added.sem, y_added.by(l, n - 1))
                    nc.scalar.activation(rows_hi[:, s % 2], rows_in[:, (s + 2) % 4], ACT.Copy)\
                        .then_inc(v_hi_made.sem, 1)

                for s in range(4):
                    v_high(s, s, 0)
                with sc.Fori(1, BLOCKS // 4) as i:
                    for s in range(4):
                        v_high(4 * i + s, s, i)
                keep_row(1)

        @block.vector
        def _(ve):
            with ve.Fori(0, L) as l:
                steps = [0]
                ve.sem_clear(dve_step.sem)

                def mark(ins):
                    ins.then_inc(dve_step.sem, 1)
                    steps[0] += 1
                    return steps[0]

                def after(n):
                    ve.wait_ge(dve_step.sem, n)

                def link(ins):
                    after(mark(ins))

                V = nc.vector

                def ada_product(n, s, place):
                    slot, before = place
                    ve.wait_ge(slot_in[slot].sem, slot_in[slot].by(l, 16 * (before + 1)))
                    if not isinstance(n, int) or n >= 2:
                        ve.wait_ge(mod_summed.sem, mod_summed.by(l, n - 1))
                    link(V.tensor_scalar(ada_sum[:, s], slots[slot][:, 0], c_t[:, 0:1], None, ALU.mult))
                    for k in range(1, K):
                        ins = V.scalar_tensor_tensor(ada_sum[:, s], slots[slot][:, k], c_t[:, k:k + 1],
                                                     ada_sum[:, s], ALU.mult, ALU.add)
                        if k < K - 1:
                            link(ins)
                    ins.then_inc(ada_summed.sem, 1)

                def modulation(n, to):
                    ve.wait_ge(mod_summed.sem, mod_summed.by(l, n + 1))
                    cols = 4 * n
                    at = slice(cols, cols + 4) if isinstance(n, int) else bass.ds(cols, 4)
                    V.tensor_tensor(mod[:, at], to[:, 0:4], par_t[:, bass.ds(l * PAR + cols, 4)], ALU.add)\
                        .then_inc(mod_made.sem, 1)

                def norm_gain(which):
                    ve.wait_ge(mod_made.sem, mod_made.by(l, N_ADA if which else N_SHIFT))
                    V.scalar_tensor_tensor(gain[:, which], mod[:, (3 * which + 1) * K:(3 * which + 2) * K], 1.0,
                                           par_t[:, bass.ds(l * PAR + (6 + which) * K, K)], ALU.add, ALU.mult)\
                        .then_inc(gain_made.sem, 1)

                def norm(which):
                    ve.wait_ge(root_made.sem, root_made.by(l, which + 1))
                    link(V.reciprocal(stat[:, 1], stat[:, 1]))
                    for b in range(TB):
                        V.tensor_scalar(x_norm[:, b], x_sb[:, b], stat[:, 1, b:b + 1], None, ALU.mult)\
                            .then_inc(normed.sem, 1)
                    if which == 0:
                        for n in range(N_SHIFT):
                            ada_product(n, n % 2, ada_place(n))
                            if n:
                                modulation(n - 1, bank[(n - 1) % 2])
                        modulation(N_SHIFT - 1, bank[(N_SHIFT - 1) % 2])
                    norm_gain(which)
                    ve.wait_ge(gain_made.sem, gain_made.by(l, which + 1))
                    for k in range(K):
                        ve.wait_ge(norm_transposed.sem, norm_transposed.by(l, 4 * which + 3 + k // 4))
                        V.tensor_scalar(h_t[:, k, P:T], bank[6 + k // 4][:, k % 4 * P:(k % 4 + 1) * P],
                                        gain[:, which, k:k + 1],
                                        mod[:, 3 * which * K + k:3 * which * K + k + 1], ALU.mult, ALU.add)\
                            .then_inc(h_t_made.sem, 1)

                norm(0)
                link(V.memset(aug[:, 0, :, :, HD + 1], 1.0))
                link(V.memset(aug[:, 1, :, :, HD], 1.0))
                ve.wait_ge(forget_summed.sem, forget_summed.by(l, 1))
                for b in range(TB):
                    mark(V.tensor_tensor(small[:, b * H:(b + 1) * H], bank[4][:, b * H:(b + 1) * H],
                                         rows_bc[:, bass.ds(l * ROWC + 2 * HD, H)], ALU.add))
                after(steps[0])
                V.scalar_tensor_tensor(small[:, 16:32], small[:, 0:16], -1.0, small[:, 0:16], ALU.mult, ALU.max)\
                    .then_inc(forget_abs.sem, 1)

                parts = [(which, b, 64 + (TB * which + b) * H) for which in range(2) for b in range(TB)]
                ada_product(N_SHIFT, 0, ada_place(N_SHIFT))
                ada_product(N_SHIFT + 1, 1, ada_place(N_SHIFT + 1))
                for n, (which, b, at) in enumerate(parts):
                    src = proj[:, b, which * COLS:(which + 1) * COLS].rearrange("p (h n) -> p h n", h=H)
                    ve.wait_ge(proj_kept.sem, proj_kept.by(l, n + 1))
                    link(V.scalar_tensor_tensor(sq_junk, src, 1.0 / HD, src, ALU.mult, ALU.mult))
                    V.tensor_reduce(small[:, at:at + H], sq_junk, AX.X, ALU.add).then_inc(qk_mean.sem, 1)
                    ve.wait_ge(qk_mean.sem, qk_mean.by(l, n + 1))
                modulation(N_SHIFT, bank[6])
                for n, (which, b, at) in enumerate(parts):
                    src = proj[:, b, which * COLS:(which + 1) * COLS].rearrange("p (h n) -> p h n", h=H)
                    ve.wait_ge(qk_root.sem, qk_root.by(l, n + 1))
                    link(V.reciprocal(small[:, at:at + H], small[:, at:at + H]))
                    link(V.scalar_tensor_tensor(src, src, HD ** -0.5 if which == 0 else 1.0,
                                                small[:, at:at + H].unsqueeze(2).to_broadcast([P, H, HD]),
                                                ALU.mult, ALU.mult))
                    link(V.tensor_tensor(aug[:, which, b, :, 0:HD], src,
                                         rows_bc[:, bass.ds(l * ROWC + which * HD, HD)].unsqueeze(1)
                                         .to_broadcast([P, H, HD]), ALU.mult))
                for n in range(N_SHIFT + 2, N_ADA):
                    ada_product(n, n % 2, ada_place(n))
                    modulation(n - 1, bank[6 + (n - 1) % 2])
                modulation(N_ADA - 1, bank[7])
                ve.wait_ge(forget_log.sem, forget_log.by(l, 2))
                V.scalar_tensor_tensor(small[:, 0:16], small[:, 0:16], 0.0, small[:, 16:32],
                                       ALU.min, ALU.subtract).then_inc(log_f_made.sem, 1)

                ve.wait_ge(cum_f_summed.sem, cum_f_summed.by(l, 1))
                cum_f = bank[5][:, 0:TB * H].rearrange("p (b h) -> p b h", h=H)
                link(V.tensor_copy(aug[:, 0, :, :, HD], cum_f))
                V.tensor_scalar(aug[:, 1, :, :, HD + 1], cum_f, -1.0, None, ALU.mult).then_inc(aug_made.sem, 1)

                def fox_maxima(h):
                    ve.wait_ge(fox_scored.sem, fox_scored.by(l, h + 1))
                    if h >= 2:
                        ve.wait_ge(fox_exp.sem, fox_exp.by(l, 2 * (h - 1)))
                    o = 40 + 2 * (h % 2)
                    mark(V.tensor_reduce(small[:, o:o + 1], bank[h % 2][:, 0:P], AX.X, ALU.max, negate=True))
                    V.tensor_reduce(small[:, o + 1:o + 2], bank[h % 2][:, P:CAUSAL], AX.X, ALU.max, negate=True)\
                        .then_inc(fox_max.sem, 1)

                def fox_normalise(h):
                    s = h % 2
                    ve.wait_ge(fox_exp.sem, fox_exp.by(l, 2 * h + 2))
                    link(V.reciprocal(small[:, 52 + 2 * s:54 + 2 * s], small[:, 48 + 2 * s:50 + 2 * s]))
                    mark(V.tensor_scalar(probs[:, s, 0:P], probs[:, s, 0:P], small[:, 52 + 2 * s:53 + 2 * s],
                                         None, ALU.mult))
                    V.tensor_scalar(probs[:, s, P:CAUSAL], probs[:, s, P:CAUSAL],
                                    small[:, 53 + 2 * s:54 + 2 * s], None, ALU.mult).then_inc(fox_probs.sem, 1)

                for h in range(H + 1):
                    if h < H:
                        fox_maxima(h)
                    if h >= 1:
                        fox_normalise(h - 1)

                def sb_softplus(h):
                    s = h % 2
                    ve.wait_ge(sb_log.sem, sb_log.by(l, 2 * h + 2))
                    if h >= 2:
                        ve.wait_ge(sb_summed.sem, sb_summed.by(l, h - 1))
                    link(V.scalar_tensor_tensor(log_keep[:, s], bank[s][:, 0:CAUSAL], 0.0, soft[:, s],
                                                ALU.max, ALU.add))
                    for n, at in enumerate((0, 2 * P)):
                        ins = V.tensor_tensor(log_keep[:, s, at:at + P], log_keep[:, s, at:at + P], sb_keep[:, :],
                                              ALU.mult)
                        if n:
                            ins.then_inc(sb_keep_made.sem, 1)
                        else:
                            mark(ins)

                for h in range(H):
                    sb_softplus(h)

                for n in range(2):
                    for b in range(TB):
                        q = 2 * n + b
                        cols = slice(n * COLS, (n + 1) * COLS)
                        other = tmp[:, (q % 2) * COLS:(q % 2 + 1) * COLS]
                        ve.wait_ge(gates_made.sem, gates_made.by(l, b + 1))
                        ve.wait_ge(branch_summed.sem, branch_summed.by(l, q + 1))
                        mark(V.tensor_tensor(merged[:, b, cols], bank[2 * (q % 2)][:, :], gates[:, b, cols],
                                             ALU.mult))
                        link(V.tensor_tensor(other, bank[2 * (q % 2) + 1][:, :],
                                             gates[:, b, D + n * COLS:D + (n + 1) * COLS], ALU.mult))
                        V.tensor_tensor(merged[:, b, cols], merged[:, b, cols], other, ALU.add)\
                            .then_inc(merged_made.sem, 1)

                ve.wait_ge(mod_made.sem, mod_made.by(l, N_ADA))

                def diagonals(which):
                    for k in range(K):
                        g = (3 * which + 2) * K + k
                        ins = V.tensor_scalar(diag[:, k], ident[:, :], mod[:, g:g + 1], None, ALU.mult)
                        if k < K - 1:
                            mark(ins)
                        else:
                            ins.then_inc(diag_made.sem, 1)

                diagonals(0)
                ve.wait_ge(row_kept.sem, row_kept.by(l, 2))
                for n in range(2):
                    for b in range(TB):
                        q = 2 * n + b
                        cols = slice(n * COLS, (n + 1) * COLS)
                        mixed = tmp[:, (q % 2) * COLS:(q % 2 + 1) * COLS]
                        ve.wait_ge(out_summed.sem, out_summed.by(l, q + 1))
                        link(V.tensor_tensor(mixed, bank[2 + q % 2][:, :], gate_row[:, cols], ALU.mult))
                        V.tensor_tensor(x_sb[:, b, cols], x_sb[:, b, cols], mixed, ALU.add).then_inc(x_mixed.sem, 1)

                ve.wait_ge(x_mixed.sem, x_mixed.by(l, 4))
                norm(1)
                ve.wait_ge(h_t_made.sem, h_t_made.by(l, 4 * K))
                ve.wait_ge(h_split.sem, h_split.by(l, 1))
                V.tensor_tensor(h_lo[:, :, :], h_t, h_hi[:, :, :].bitcast(F32), ALU.subtract).then_inc(h_split.sem, 1)

                def top16(rows, top, at):
                    n = len(rows)
                    cost = 0.06 + rows[0].shape[1] / 960
                    first = steps[0]
                    for r in range(n):
                        mark(V.max(top[:, r, 0:8], rows[r]))
                        yield cost
                    for r in range(n):
                        after(first + r + 1)
                        mark(V.max_index(at[:, r, 0:8], top[:, r, 0:8], rows[r]))
                        yield cost
                    for r in range(n):
                        after(first + n + r + 1)
                        mark(V.match_replace(rows[r], top[:, r, 0:8], rows[r], LOWEST))
                        yield cost
                    for r in range(n):
                        after(first + 2 * n + r + 1)
                        mark(V.max(top[:, r, 8:16], rows[r]))
                        yield cost
                    for r in range(n):
                        after(first + 3 * n + r + 1)
                        mark(V.max_index(at[:, r, 8:16], top[:, r, 8:16], rows[r]))
                        yield cost
                    after(steps[0])

                def route(b):
                    ve.wait_ge(scores_kept.sem, scores_kept.by(l, 3 * (b + 1)))
                    ve.wait_ge(scored.sem, scored.by(l, 4 * (b + 1)))
                    V.tensor_copy(score[:, b, 12:16], score_bank(b, 3)).then_inc(last_scores_kept.sem, 1)
                    link(V.memset(small[:, 0:1], 0.0))
                    yield 0.7
                    yield from top16([score[:, b, r] for r in range(2 * H)], top1, top1_at)
                    mark(V.tensor_copy(top1_f, top1_at))
                    both = top1.rearrange("p (w h) k -> p h w k", w=2)
                    for h in range(H):
                        mark(V.tensor_tensor(cand[:, h], both[:, h, 0].unsqueeze(2).to_broadcast([P, TOPK, TOPK]),
                                             both[:, h, 1].unsqueeze(1).to_broadcast([P, TOPK, TOPK]), ALU.add))
                        yield 0.33
                    after(steps[0])
                    yield from top16([cand_words[:, h * 256:(h + 1) * 256] for h in range(H)], top2[:, b],
                                     top2_at[:, b].rearrange("p (h k) -> p h k", k=TOPK))
                    link(V.tensor_reduce(small[:, 0:H], top2[:, b], AX.X, ALU.max))
                    V.tensor_tensor(top2[:, b], top2[:, b], small[:, 0:H].unsqueeze(2).to_broadcast([P, H, TOPK]),
                                    ALU.subtract).then_inc(soft_sub.sem, 1)
                    ve.wait_ge(soft_sub.sem, soft_sub.by(l, b + 1))
                    yield 0.4
                    which_f = top1_f.rearrange("p (w h) k -> p h w k", w=2)
                    for w in range(2):
                        if w == 0:
                            link(V.tensor_single_scalar(digit, top2_at[:, b], 4, ALU.logical_shift_right))
                        else:
                            link(V.tensor_single_scalar(digit, top2_at[:, b], TOPK - 1, ALU.bitwise_and))
                        link(V.tensor_copy(digit_f, digit))
                        yield 0.3
                        link(V.tensor_tensor(onehot, digit_f.unsqueeze(2).to_broadcast([P, PAIRS, TOPK]),
                                             iota[:, 0:TOPK].unsqueeze(1).to_broadcast([P, PAIRS, TOPK]),
                                             ALU.is_equal))
                        yield 2.2
                        for h in range(H):
                            one = onehot[:, h * TOPK:(h + 1) * TOPK]
                            mark(V.tensor_tensor(one, one, which_f[:, h, w].unsqueeze(1)
                                                 .to_broadcast([P, TOPK, TOPK]), ALU.mult))
                            yield 0.33
                        after(steps[0])
                        link(V.tensor_reduce(routed[:, b, 1 - w], onehot, AX.X, ALU.add))
                        yield 2.2

                def ut_low(n, s, wait=True):
                    if wait:
                        ve.wait_ge(act_summed.sem, act_summed.by(l, n - 1))
                    for half in range(2):
                        cols = slice(half * COLS, (half + 1) * COLS)
                        ve.wait_ge(ut_hi_made.sem, ut_hi_made.by(l, 2 * n + half + 1))
                        V.tensor_tensor(rows_lo[:, s, cols], ut_bank[half][:, :], rows_hi[:, s, cols].bitcast(F32),
                                        ALU.subtract).then_inc(ut_lo_made.sem, 1)

                split, spent = 0, 0.0
                for b in range(TB):
                    for cost in route(b):
                        spent += cost
                        if spent > BETWEEN and split < EARLY:
                            ut_low(split, split % 2, wait=split >= 2)
                            split, spent = split + 1, 0.0
                for n in range(split, EARLY + 1):
                    ut_low(n, n % 2)
                ve.wait_ge(soft_exp.sem, soft_exp.by(l, 1))
                for b in range(TB):
                    link(V.tensor_reduce(small[:, 8:8 + H], top2[:, b], AX.X, ALU.add))
                    link(V.reciprocal(small[:, 16:16 + H], small[:, 8:8 + H]))
                    ins = V.tensor_tensor(routed[:, b, 2].rearrange("p (h k) -> p h k", k=TOPK), top2[:, b],
                                          small[:, 16:16 + H].unsqueeze(2).to_broadcast([P, H, TOPK]), ALU.mult)
                    if b == 0:
                        link(ins)
                    else:
                        ins.then_inc(route_made.sem, 1)

                def one_hots(g, s, first=False):
                    if first:
                        ve.wait_ge(route_kept.sem, route_kept.by(l, TB))
                    else:
                        ve.wait_ge(gates_summed.sem, gates_summed.by(l, g - 1))
                    at = slice(g * GROUP, (g + 1) * GROUP) if first else bass.ds(g * GROUP, GROUP)
                    V.tensor_tensor(hot2[:, s * GROUP:(s + 1) * GROUP],
                                    iota[:, :].unsqueeze(1).to_broadcast([P, GROUP, P]),
                                    route_t[:, 0, at].unsqueeze(2).to_broadcast([P, GROUP, P]), ALU.is_equal)
                    for j in range(GROUP):
                        t = g * GROUP + j
                        ins = V.tensor_scalar(hot1[:, s * GROUP + j], iota[:, :], route_t[:, 1, bass.ds(t, 1)],
                                              route_t[:, 2, bass.ds(t, 1)], ALU.is_equal, ALU.mult)
                    ins.then_inc(hot_made.sem, 1)

                def gate_blocks(g, j):
                    ve.wait_ge(gates_kept.sem, gates_kept.by(l, g + 1))
                    at = slice(g * GROUP, (g + 1) * GROUP) if isinstance(g, int) else bass.ds(g * GROUP, GROUP)
                    to = weight[:, 0:LATE_AT, at].rearrange("p e t -> p t e")
                    V.tensor_tensor(to, to, gate_bank[j][:, :].rearrange("p (t e) -> p t e", t=GROUP)[:, :, 0:LATE_AT],
                                    ALU.mult).then_inc(gates_used.sem, 1)

                def weigh(n, s):
                    ve.wait_ge(act_made.sem, act_made.by(l, n + 1))
                    to = weight[:, n] if isinstance(n, int) else weight[:, bass.ds(n, 1)].squeeze(1)
                    V.tensor_tensor(to, to, act[:, s], ALU.mult).then_inc(weight_made.sem, 1)

                def gates_and_block(i, m, first=False, last=False):
                    n = EARLY + 2 * i + m
                    for j in (2 * m, 2 * m + 1):
                        g = 4 * i + j
                        if not last:
                            one_hots(g + 2, j % 2)
                        if not first and not (isinstance(i, int) and i == 0 and m == 1):
                            ve.wait_ge(weight_made.sem, weight_made.by(l, n - 1 - EARLY))
                        gate_blocks(g, j)
                    ut_low(n + 1, 1 - m)
                    if not first:
                        ve.wait_ge(gates_used.sem, gates_used.by(l, 4 * i + 2 * m + 2))
                        weigh(n - 1, 1 - m)

                ve.wait_ge(act_made.sem, act_made.by(l, EARLY))
                ve.wait_ge(ones_laid.sem, ones_laid.by(l, 2))
                for s in range(2):
                    one_hots(s, s, True)
                gates_and_block(0, 0, first=True)
                gates_and_block(0, 1)
                with ve.Fori(1, MIDDLE // 2 - 1) as i:
                    for m in range(2):
                        gates_and_block(i, m)
                gates_and_block(MIDDLE // 2 - 1, 0)
                gates_and_block(MIDDLE // 2 - 1, 1, last=True)
                ve.wait_ge(gates_used.sem, gates_used.by(l, N_GROUPS))
                weigh(LATE_AT - 1, 1)
                ve.wait_ge(gates_kept.sem, gates_kept.by(l, N_GROUPS))
                ut_low(LATE_AT + 1, 1)
                with ve.Fori(LATE_AT // 2, BLOCKS // 2 - 1) as i:
                    for s in range(2):
                        weigh(2 * i + s, s)
                        ut_low(2 * i + s + 2, s)
                for s in range(2):
                    weigh(BLOCKS - 2 + s, s)

                def split_weights(n, s4):
                    s = s4 % 2
                    if not isinstance(n, int) or n >= 2:
                        ve.wait_ge(y_added.sem, y_added.by(l, n - 1))
                    of = weight[:, n] if isinstance(n, int) else weight[:, bass.ds(n, 1)].squeeze(1)
                    V.tensor_copy(w_hi[:, s], of).then_inc(w_hi_made.sem, 1)
                    ve.wait_ge(w_hi_made.sem, w_hi_made.by(l, n + 1))
                    V.tensor_tensor(w_lo[:, s], of, w_hi[:, s].bitcast(F32), ALU.subtract).then_inc(w_split.sem, 1)
                    ve.wait_ge(v_hi_made.sem, v_hi_made.by(l, n + 1))
                    V.tensor_tensor(rows_lo[:, s], rows_in[:, (s4 + 2) % 4], rows_hi[:, s].bitcast(F32),
                                    ALU.subtract).then_inc(v_split.sem, 1)

                ve.wait_ge(gates_used.sem, gates_used.by(l, N_GROUPS))
                ve.wait_ge(weight_made.sem, weight_made.by(l, BLOCKS - EARLY))
                for s in range(4):
                    split_weights(s, s)
                in_slots = (K * T + 2 * K * COLS) // T
                with ve.Fori(1, in_slots // 4) as i:
                    for s in range(4):
                        split_weights(4 * i + s, s)
                ve.wait_ge(w_split.sem, w_split.by(l, in_slots))
                V.memset(small[:, 0:1], 0.0).then_inc(slots_free.sem, 1)
                with ve.Fori(in_slots // 4, BLOCKS // 4) as i:
                    for s in range(4):
                        split_weights(4 * i + s, s)

                diagonals(1)
                ve.wait_ge(row_kept.sem, row_kept.by(l, 4))
                ve.wait_ge(y_added.sem, y_added.by(l, BLOCKS))
                for b in range(TB):
                    for n in range(2):
                        q = 2 * b + n
                        cols = slice(n * COLS, (n + 1) * COLS)
                        gated = tmp[:, (q % 2) * COLS:(q % 2 + 1) * COLS]
                        link(V.tensor_tensor(gated, y_bank[q][:, :], gate_row[:, cols], ALU.mult))
                        V.tensor_tensor(x_sb[:, b, cols], x_sb[:, b, cols], gated, ALU.add).then_inc(x_done.sem, 1)
                ve.wait_ge(x_done.sem, x_done.by(l, 4))
                V.memset(small[:, 0:1], 0.0).then_inc(arena_free.sem, 1)

        @block.tensor
        def _(pe):
            M = nc.tensor
            pe.wait_ge(masks_made.sem, MASKS)
            pe.wait_ge(inputs_in.sem, 16 * 14)
            M.transpose(bank[0][:, 0:P], par_rows, ident[:, :]).then_inc(setup_transposed.sem, 1)
            M.transpose(bank[1][:, 0:K], c_rows, ident[0:K, 0:K]).then_inc(setup_transposed.sem, 1)
            M.matmul(bank[2][:, 0:L * ROWC], ones[0:1, :], row_consts, start=True, stop=True)\
                .then_inc(setup_transposed.sem, 1)
            pe.wait_ge(setup_done.sem, 3)
            pe.nop().then_inc(arena_free.sem, 1)
            pe.nop().then_inc(slots_free.sem, 1)

            with pe.Fori(0, L) as l:
                def norm(which):
                    for b in range(TB):
                        pe.wait_ge(normed.sem, normed.by(l, TB * which + b + 1))
                        for k in range(K):
                            ins = M.transpose(bank[4 + 2 * b + k // 4][:, k % 4 * P:(k % 4 + 1) * P],
                                              x_norm[:, b, k * P:(k + 1) * P], ident[:, :])
                            if k % 4 == 3:
                                ins.then_inc(norm_transposed.sem, 1)

                def modulate(n, s, to):
                    pe.wait_ge(ada_summed.sem, ada_summed.by(l, n + 1))
                    for j in range(COLS // P):
                        ins = M.matmul(to[:, j:j + 1], ada_sum[:, s, j * P:(j + 1) * P], ones[:, 0:1],
                                       start=True, stop=True)
                    ins.then_inc(mod_summed.sem, 1)

                norm(0)
                for n in range(N_SHIFT):
                    if n >= 2:
                        pe.wait_ge(mod_made.sem, mod_made.by(l, n - 1))
                    modulate(n, n % 2, bank[n % 2])
                pe.wait_ge(h_t_made.sem, h_t_made.by(l, 2 * K))
                pe.wait_ge(forget_w_in.sem, forget_w_in.by(l, 16))
                for b in range(TB):
                    for k in range(K):
                        ins = M.matmul(bank[4][:, b * H:(b + 1) * H], h_t[:, k, b * P:(b + 1) * P], forget_w[:, k],
                                       start=k == 0, stop=k == K - 1)
                ins.then_inc(forget_summed.sem, 1)

                def weights_in(n):
                    slot, before = weight_place(n)
                    pe.wait_ge(slot_in[slot].sem, slot_in[slot].by(l, 16 * (before + 1)))
                    return slots[slot]

                def project(n):
                    w = weights_in(n)
                    for b in range(TB):
                        if n < 2:
                            pe.wait_ge(mod_made.sem, mod_made.by(l, N_SHIFT))
                        else:
                            pe.wait_ge(proj_kept.sem, proj_kept.by(l, 2 * (n - 2) + b + 1))
                        for k in range(K):
                            ins = M.matmul(bank[2 * (n % 2) + b][:, :], h_t[:, k, b * P:(b + 1) * P], w[:, k],
                                           start=k == 0, stop=k == K - 1)
                        ins.then_inc(proj_summed.sem, 1)

                for n in range(N_PROJ):
                    project(n)
                    m = N_SHIFT + n - 2
                    if N_SHIFT <= m < N_ADA:
                        if m >= N_SHIFT + 2:
                            pe.wait_ge(mod_made.sem, mod_made.by(l, m - 1))
                        modulate(m, m % 2, bank[6 + m % 2])

                pe.wait_ge(log_f_made.sem, log_f_made.by(l, 1))
                M.matmul(bank[5][:, 0:H], cumsum_tri[:, :], small[:, 0:H], start=True, stop=True)
                M.matmul(bank[5][:, H:2 * H], cumsum_tri[:, :], small[:, H:2 * H], start=True, stop=False)
                M.matmul(bank[5][:, H:2 * H], ones[:, :], small[:, 0:H], start=False, stop=True)\
                    .then_inc(cum_f_summed.sem, 1)
                pe.wait_ge(aug_made.sem, aug_made.by(l, 1))
                pe.wait_ge(proj_kept.sem, proj_kept.by(l, TB * N_PROJ))
                pe.wait_ge(mod_made.sem, mod_made.by(l, N_ADA))

                def turn_qk(n):
                    if n >= 2:
                        pe.wait_ge(qk_kept.sem, qk_kept.by(l, n - 1))
                    for which in range(2):
                        for b in range(TB):
                            cols = slice((2 * which + b) * P, (2 * which + b + 1) * P)
                            if n < H:
                                ins = M.transpose(bank[4 + n % 2][0:AUG, cols], aug[:, which, b, n], ident[:, :])
                            else:
                                at = (3 + which) * COLS + (n - H) * P
                                ins = M.transpose(bank[4 + n % 2][:, cols], proj[:, b, at:at + P], ident[:, :])
                    ins.then_inc(qk_turned.sem, 1)

                def fox_scores(h):
                    pe.wait_ge(qk_kept.sem, qk_kept.by(l, h + 1))
                    if h >= 2:
                        pe.wait_ge(fox_exp.sem, fox_exp.by(l, 2 * (h - 1)))
                    q, k = fox_qk[0:AUG, h, 0:T], fox_qk[0:AUG, h, T:2 * T]
                    to = bank[h % 2]
                    M.matmul(to[:, 0:P], q[:, 0:P], k[:, 0:P], start=True, stop=False)
                    M.matmul(to[:, 0:P], ident[:, :], fox_mask[:, :], start=False, stop=True)
                    M.matmul(to[:, P:CAUSAL], q[:, P:T], k[:, 0:T], start=True, stop=False)
                    M.matmul(to[:, 2 * P:CAUSAL], ident[:, :], fox_mask[:, :], start=False, stop=True)\
                        .then_inc(fox_scored.sem, 1)

                def turn_probs(h):
                    pe.wait_ge(fox_probs.sem, fox_probs.by(l, h + 1))
                    if h >= 2:
                        pe.wait_ge(probs_kept.sem, probs_kept.by(l, h - 1))
                    for n in range(3):
                        ins = M.transpose(bank[2 + h % 2][:, n * P:(n + 1) * P],
                                          probs[:, h % 2, n * P:(n + 1) * P], ident[:, :])
                    ins.then_inc(probs_turned.sem, 1)

                def values(h, group):
                    n = group * H // 2 + h // 2
                    if n >= 2 and h % 2 == 0:
                        pe.wait_ge(y_kept.sem, y_kept.by(l, n - 1))
                    to = bank[6 + n % 2][h % 2 * HD:(h % 2 + 1) * HD, :]
                    at = (2 + 3 * group) * COLS + h * HD
                    M.matmul(to[:, 0:T], proj[:, 0, at:at + HD], probs_t[:, h % 2, 0:T], start=True, stop=False)
                    ins = M.matmul(to[:, P:T], proj[:, 1, at:at + HD], probs_t[:, h % 2, T:CAUSAL],
                                   start=False, stop=True)
                    if h % 2:
                        ins.then_inc(y_summed.sem, 1)

                turn_qk(0)
                turn_qk(1)
                for h in range(H + 2):
                    if h < H:
                        fox_scores(h)
                        turn_qk(h + 2)
                    if 1 <= h <= H:
                        turn_probs(h - 1)
                    if h >= 2:
                        pe.wait_ge(probs_kept.sem, probs_kept.by(l, h - 1))
                        values(h - 2, 0)
                turn_qk(H + 2)
                turn_qk(H + 3)

                def sb_scores(h, to, stop):
                    half = slice(h % 2 * HD, (h % 2 + 1) * HD)
                    q, k = sb_qk[half, h // 2, 0:T], sb_qk[half, h // 2, T:2 * T]
                    for b in range(2):
                        ins = M.matmul(to[:, 2 * b * P:2 * b * P + T - b * P], k[:, b * P:(b + 1) * P],
                                       q[:, b * P:T], start=True, stop=stop)
                        yield b, ins

                def sb_z(h):
                    pe.wait_ge(qk_kept.sem, qk_kept.by(l, H + h // 2 + 1))
                    if h >= 2:
                        pe.wait_ge(sb_keep_made.sem, sb_keep_made.by(l, h - 1))
                    for _, ins in sb_scores(h, bank[h % 2], True):
                        pass
                    ins.then_inc(sb_scored.sem, 1)

                def sb_logits(h):
                    keep = log_keep[:, h % 2]
                    to = bank[2 + h % 2]
                    pe.wait_ge(sb_keep_made.sem, sb_keep_made.by(l, h + 1))
                    if h >= 2:
                        pe.wait_ge(sb_weights.sem, sb_weights.by(l, h - 1))
                    for b, _ in sb_scores(h, to, False):
                        if b == 0:
                            M.matmul(to[:, 0:T], neg_suffix_tri[:, :], keep[:, 0:T], start=False, stop=False)
                            M.matmul(to[:, P:T], neg_ones[:, :], keep[:, T:CAUSAL], start=False, stop=False)
                            M.matmul(to[:, 0:P], ident[:, :], sb_mask[:, :], start=False, stop=True)
                        else:
                            M.matmul(to[:, T:CAUSAL], neg_suffix_tri[:, :], keep[:, T:CAUSAL],
                                     start=False, stop=False)
                            M.matmul(to[:, T:CAUSAL], ident[:, :], sb_mask[:, :], start=False, stop=True)\
                                .then_inc(sb_summed.sem, 1)

                for h in range(H + 2):
                    if h < H:
                        sb_z(h)
                    if 1 <= h <= H:
                        sb_logits(h - 1)
                    if h >= 2:
                        pe.wait_ge(sb_weights.sem, sb_weights.by(l, h - 1))
                        values(h - 2, 1)

                pe.wait_ge(y_kept.sem, y_kept.by(l, H))
                for n in range(2):
                    w = weights_in(AT_BRANCH + n)
                    for b in range(TB):
                        q = 2 * n + b
                        if q >= 2:
                            pe.wait_ge(merged_made.sem, merged_made.by(l, q - 1))
                        for g in range(2):
                            for k in range(4):
                                ins = M.matmul(bank[2 * (q % 2) + g][:, :], y_t[:, 4 * g + k, b * P:(b + 1) * P],
                                               w[:, 4 * g + k], start=k == 0, stop=k == 3)
                        ins.then_inc(branch_summed.sem, 1)

                for n in range(4):
                    b, half = n // 2, n % 2
                    if half == 0:
                        pe.wait_ge(merged_made.sem, merged_made.by(l, 3 + b))
                    for j in range(4):
                        k = 4 * half + j
                        ins = M.transpose(bank[4 + n][:, j * P:(j + 1) * P], merged[:, b, k * P:(k + 1) * P],
                                          ident[:, :])
                    ins.then_inc(merged_turned.sem, 1)

                def gate_rows(which):
                    pe.wait_ge(diag_made.sem, diag_made.by(l, which + 1))
                    for k in range(K):
                        to = bank[(0 if which == 0 else 4) + k // 4]
                        ins = M.matmul(to[:, k % 4 * P:(k % 4 + 1) * P], ones[:, :], diag[:, k],
                                       start=True, stop=True)
                        if k % 4 == 3:
                            ins.then_inc(row_summed.sem, 1)

                gate_rows(0)
                for n in range(2):
                    w = weights_in(AT_OUT + n)
                    for b in range(TB):
                        q = 2 * n + b
                        pe.wait_ge(merged_kept.sem, merged_kept.by(l, 2 * b + 2))
                        if q >= 2:
                            pe.wait_ge(x_mixed.sem, x_mixed.by(l, q - 1))
                        for k in range(K):
                            ins = M.matmul(bank[2 + q % 2][:, :], h_t[:, k, b * P:(b + 1) * P], w[:, k],
                                           start=k == 0, stop=k == K - 1)
                        ins.then_inc(out_summed.sem, 1)

                norm(1)
                pe.wait_ge(h_t_made.sem, h_t_made.by(l, 4 * K))
                for h in range(H):
                    if h % 4 == 0:
                        w = weights_in(AT_WQ + h // 4)
                    if h >= 2:
                        pe.wait_ge(pq_kept.sem, pq_kept.by(l, h - 1))
                    for k in range(K):
                        ins = M.matmul(bank[h % 2][:, 0:T], w[:, k, h % 4 * P:(h % 4 + 1) * P], h_t[:, k],
                                       start=k == 0, stop=k == K - 1)
                    ins.then_inc(pq_summed.sem, 1)
                pe.wait_ge(keys_in.sem, keys_in.by(l, 32))
                for h in range(H):
                    ins = M.transpose(bank[2 + h // 4][:, h % 4 * P:(h % 4 + 1) * P], keys[:, h], ident[:, :])
                    if h % 4 == 3:
                        ins.then_inc(keys_turned.sem, 1)
                pe.wait_ge(keys_kept.sem, keys_kept.by(l, 2))
                pe.wait_ge(pq_kept.sem, pq_kept.by(l, H))
                for b in range(TB):
                    for n in range(4):
                        w, g = n % 2, n // 2
                        half = slice(w * HD, (w + 1) * HD)
                        for j in range(4):
                            h = 4 * g + j
                            ins = M.matmul(bank[(4 if b == 0 else 0) + 2 * w + g][:, j * P:(j + 1) * P],
                                           pq_t[half, h, b * P:(b + 1) * P], keys_t[half, h],
                                           start=True, stop=True)
                        ins.then_inc(scored.sem, 1)

                def turn_u(n, s, i, first=False):
                    pe.wait_ge(u_landed[s].sem, u_landed[s].by(l, 16 * i + 16))
                    for half in range(2):
                        if not first:
                            pe.wait_ge(ut_lo_made.sem, ut_lo_made.by(l, 2 * (n - 1) + half + 1))
                        for j in range(4):
                            k = 4 * half + j
                            ins = M.transpose(ut_bank[half][:, j * P:(j + 1) * P],
                                              rows_in[:, s, k * P:(k + 1) * P], ident[:, :])
                        ins.then_inc(ut_turned.sem, 1)

                def inputs_sum(n, s, wait=True):
                    pe.wait_ge(ut_lo_made.sem, ut_lo_made.by(l, 2 * n + 2))
                    if wait:
                        pe.wait_ge(act_made.sem, act_made.by(l, n - 1))
                    for k in range(K):
                        hi, lo = rows_hi[:, s, k * P:(k + 1) * P], rows_lo[:, s, k * P:(k + 1) * P]
                        to = act_bank[s][:, 0:T]
                        M.matmul(to, hi, h_hi[:, k], start=k == 0, stop=False)
                        M.matmul(to, hi, h_lo[:, k], start=False, stop=False)
                        ins = M.matmul(to, lo, h_hi[:, k], start=False, stop=k == K - 1)
                    ins.then_inc(act_summed.sem, 1)

                pe.wait_ge(scores_kept.sem, scores_kept.by(l, 3))
                pe.wait_ge(last_scores_kept.sem, last_scores_kept.by(l, 1))
                turn_u(0, 0, 0, first=True)
                pe.wait_ge(h_split.sem, h_split.by(l, 2))
                turn_u(1, 1, 0)
                inputs_sum(0, 0, wait=False)
                turn_u(2, 0, 1)
                inputs_sum(1, 1, wait=False)
                with pe.Fori(1, EARLY // 2) as i:
                    turn_u(2 * i + 1, 1, i)
                    inputs_sum(2 * i, 0)
                    turn_u(2 * i + 2, 0, i + 1)
                    inputs_sum(2 * i + 1, 1)
                pe.wait_ge(scores_kept.sem, scores_kept.by(l, 3 * TB))
                pe.wait_ge(route_made.sem, route_made.by(l, 1))
                for b in range(TB):
                    for w in range(3):
                        ins = M.transpose(bank[b][:, w * P:(w + 1) * P], routed[:, b, w], ident[:, :])
                    ins.then_inc(route_turned.sem, 1)

                def token_gates(g, j, first=False):
                    pe.wait_ge(hot_made.sem, hot_made.by(l, g + 1))
                    if not first:
                        pe.wait_ge(gates_used.sem, gates_used.by(l, g - 3))
                    for t in range(GROUP):
                        at = j % 2 * GROUP + t
                        ins = M.matmul(gate_bank[j][:, t * P:(t + 1) * P], hot2[:, at], hot1[:, at],
                                       start=True, stop=True)
                    ins.then_inc(gates_summed.sem, 1)

                def gates_and_block(i, m, first=False):
                    n = EARLY + 2 * i + m
                    for j in (2 * m, 2 * m + 1):
                        token_gates(4 * i + j, j, first)
                    turn_u(n + 1, 1 - m, EARLY // 2 + i + m)
                    inputs_sum(n, m)

                pe.wait_ge(route_kept.sem, route_kept.by(l, TB))
                pe.wait_ge(last_scores_kept.sem, last_scores_kept.by(l, TB))
                for m in range(2):
                    gates_and_block(0, m, first=True)
                with pe.Fori(1, MIDDLE // 2) as i:
                    for m in range(2):
                        gates_and_block(i, m)
                turn_u(LATE_AT + 1, 1, LATE_AT // 2)
                with pe.Fori(LATE_AT // 2, BLOCKS // 2 - 1) as i:
                    for s in range(2):
                        inputs_sum(2 * i + s, s)
                        turn_u(2 * i + s + 2, s, i + 1)
                inputs_sum(BLOCKS - 2, 0)
                inputs_sum(BLOCKS - 1, 1)

                def outputs_add(n, s, start=False, stop=False):
                    pe.wait_ge(w_split.sem, w_split.by(l, n + 1))
                    pe.wait_ge(v_hi_made.sem, v_hi_made.by(l, n + 1))
                    for part_no, (w, v) in enumerate(((w_hi, rows_hi), (w_lo, rows_hi), (w_hi, rows_lo))):
                        if part_no == 2:
                            pe.wait_ge(v_split.sem, v_split.by(l, n + 1))
                        for b in range(TB):
                            for half in range(2):
                                ins = M.matmul(y_bank[2 * b + half][:, :], w[:, s, b * P:(b + 1) * P],
                                               v[:, s, half * COLS:(half + 1) * COLS],
                                               start=start and part_no == 0, stop=stop and part_no == 2)
                    ins.then_inc(y_added.sem, 1)

                pe.wait_ge(gates_used.sem, gates_used.by(l, N_GROUPS))
                outputs_add(0, 0, start=True)
                outputs_add(1, 1)
                with pe.Fori(1, BLOCKS // 2 - 1) as i:
                    for s in range(2):
                        outputs_add(2 * i + s, s)
                outputs_add(BLOCKS - 2, 0)
                outputs_add(BLOCKS - 1, 1, stop=True)
                gate_rows(1)


_INS = ['x', 'c', 'ada_w', 'ada_b', 'attn_norm', 'ffn_norm', 'w_in', 'fox_bf', 'fox_q_gain', 'fox_k_gain',
        'w_branch', 'w_out', 'peer_wq', 'peer_k1', 'peer_k2', 'peer_u', 'peer_v']


def kernel(**inputs):
    import numpy as np
    import concourse.bacc as bacc
    from concourse.bass_utils import run_bass_kernel_spmd

    nc = bacc.Bacc("TRN2", target_bir_lowering=False, num_devices=1)
    arrays, args = {}, []
    for name in _INS:
        a = np.ascontiguousarray(inputs[name])
        arrays[f"in_{name}"] = a
        args.append(nc.dram_tensor(f"in_{name}", a.shape, mybir.dt.from_np(a.dtype), kind="ExternalInput").ap())
    out = nc.dram_tensor("out", (1, T, D), F32, kind="ExternalOutput").ap()
    hybrid_fox_stickbreak_peer(nc, *args, out)
    r = run_bass_kernel_spmd(nc, [arrays], core_ids=[0])
    return r.results[0]["out"]
```

```python
from contextlib import ExitStack

import concourse.bass as bass
from concourse import mybir

ALU = mybir.AluOpType
ACT = mybir.ActivationFunctionType
AX = mybir.AxisListType
F32 = mybir.dt.float32
F32R = mybir.dt.float32r
U32 = mybir.dt.uint32

P = 128
D = 1024
T = 256
L = 2
H = 8
HD = 64
KEYS = 128
TOPK = 16
PAIRS = H * TOPK
EPS = 1e-6
NEG = -1e30
LOWEST = -3e38

TB = T // P
K = D // P
COLS = 512
IN_WIDTH = 5128
FA = 3 * H * HD
N_ADA = 6 * D // COLS
N_PROJ = (IN_WIDTH - H) // COLS
N_BRANCH = N_OUT = N_WQ = D // COLS
N_WEIGHTS = N_PROJ + N_BRANCH + N_OUT + N_WQ
N_SHIFT = 2 * D // COLS
N_LATER = N_ADA - N_SHIFT
AT_BRANCH = N_PROJ
AT_OUT = AT_BRANCH + N_BRANCH
AT_WQ = AT_OUT + N_OUT
SHIFT_LOADS = (56, 60, 76, 84)
SHIFT_PRODUCTS = (64, 72, 80, 88)
ROWS_AT = 104
BLOCKS = KEYS
EARLY = 64
MIDDLE = 32
LATE_AT = EARLY + MIDDLE
ROUTED = 56
GROUP = 4
N_GROUPS = T // GROUP
CAUSAL = 3 * P
AUG = HD + 2

PAR = 6 * K + 2 * K
ROWC = 2 * HD + H


class Signal:

    def __init__(self, ctx, nc, name, per_layer=0):
        self.sem = ctx.enter_context(nc.semaphore(name))
        self.per_layer = per_layer

    def by(self, layer, count):
        return layer * self.per_layer + count


def hybrid_fox_stickbreak_peer(nc, x, c, ada_w, ada_b, attn_norm, ffn_norm, w_in, fox_bf, fox_q_gain,
                               fox_k_gain, w_branch, w_out, peer_wq, peer_k1, peer_k2, peer_u, peer_v, out):
    ctx = ExitStack()
    with ctx:
        def sb(name, shape, dt=F32):
            return ctx.enter_context(nc.sbuf_tensor(name, shape, dt))

        x_sb = sb("x_sb", [P, TB, D])
        ident = sb("ident", [P, P])
        ones = sb("ones", [P, P])
        neg_ones = sb("neg_ones", [P, P])
        cumsum_tri = sb("cumsum_tri", [P, P])
        neg_suffix_tri = sb("neg_suffix_tri", [P, P])
        ident_r = sb("ident_r", [P, P], F32R)
        fox_mask = sb("fox_mask", [P, CAUSAL], F32R)
        sb_mask = sb("sb_mask", [P, CAUSAL], F32R)
        iota = sb("iota", [P, P])
        par_t = sb("par_t", [P, L * PAR])
        c_t = sb("c_t", [P, K])
        rows_bc = sb("rows_bc", [P, L * ROWC])
        mod = sb("mod", [P, 6 * K])
        gain = sb("gain", [P, 2, K])
        stat = sb("stat", [P, 2, TB])
        small = sb("small", [P, 96])
        eps = sb("eps", [P, 1])
        h_hi = sb("h_hi", [P, K, T], F32R)
        h_lo = sb("h_lo", [P, K, T], F32R)
        rows_in = sb("rows_in", [P, 4, D])
        rows_hi = sb("rows_hi", [P, 2, D], F32R)
        rows_lo = sb("rows_lo", [P, 2, D], F32R)
        ada_sum = sb("ada_sum", [P, 2, COLS])
        act = sb("act", [P, 2, T])
        w_hi = sb("w_hi", [P, 2, T], F32R)
        w_lo = sb("w_lo", [P, 2, T], F32R)
        route_t = sb("route_t", [P, 3, T])
        hot2 = rows_in[:, 2, :].rearrange("p (t n) -> p t n", n=P)
        hot1 = rows_in[:, 3, :].rearrange("p (t n) -> p t n", n=P)
        par_rows = rows_in[:, 0, 0:P]
        c_rows = rows_in[0:K, 0, P:2 * P]
        row_consts = rows_in[0:1, 0, 2 * P:2 * P + L * ROWC]

        arena = sb("arena", [P, T * KEYS])
        weight = arena[:, :].rearrange("p (e t) -> p e t", t=T)
        cursor = [0]

        def part(words):
            cursor[0] += words
            return arena[:, cursor[0] - words:cursor[0]]

        mask_rows = arena[:, 0:2 * CAUSAL].rearrange("p (w n) -> p w n", w=2)
        h_t = part(K * T).rearrange("p (k t) -> p k t", k=K)
        w_slot = part(2 * K * COLS).rearrange("p (s k n) -> p s k n", s=2, k=K)
        slots = [w_slot[:, 0], w_slot[:, 1], rows_in[:, :, :].rearrange("p a (k n) -> p (a k) n", n=COLS)]
        qk_words = part(H * COLS + H // 2 * COLS)
        y_words = part(2 * 4 * T)
        aug_words = part(2 * TB * H * AUG)
        tmp = part(T * KEYS - TB * N_PROJ * COLS - cursor[0])
        proj_words = part(TB * N_PROJ * COLS)
        proj = proj_words.rearrange("p (b n) -> p b n", b=TB)
        fox_qk = qk_words[:, 0:H * COLS].rearrange("p (h n) -> p h n", h=H)
        sb_qk = qk_words[:, H * COLS:].rearrange("p (h n) -> p h n", h=H // 2)
        x_norm = qk_words[:, 0:TB * D].rearrange("p (b n) -> p b n", b=TB)
        junk = qk_words[:, 4096:4096 + D]
        sq_junk = qk_words[:, 4096 + D:4096 + D + COLS].rearrange("p (h n) -> p h n", h=H)
        merged = qk_words[:, 0:TB * D].rearrange("p (b n) -> p b n", b=TB)
        pq_t = qk_words[:, TB * D:TB * D + H * T].rearrange("p (h t) -> p h t", h=H)
        gate_row = y_words[:, 0:D]
        aug = aug_words.rearrange("p (w b h e) -> p w b h e", w=2, b=TB, h=H)
        diag = aug_words[:, 0:D].rearrange("p (k n) -> p k n", k=K)
        keys = aug_words[:, D:D + H * P].rearrange("p (h n) -> p h n", h=H)
        probs = tmp[:, 0:2 * CAUSAL].rearrange("p (s n) -> p s n", s=2)
        probs_t = tmp[:, 2 * CAUSAL:4 * CAUSAL].rearrange("p (s n) -> p s n", s=2)
        keys_t = tmp[:, 0:H * P].rearrange("p (h n) -> p h n", h=H)
        forget_w = tmp[:, 4 * CAUSAL:4 * CAUSAL + K * H].rearrange("p (k n) -> p k n", k=K)
        soft = proj[:, 0, 0:2 * CAUSAL].rearrange("p (s n) -> p s n", s=2)
        log_keep = proj[:, 1, 0:2 * CAUSAL].rearrange("p (s n) -> p s n", s=2)
        gates = proj[:, :, 6 * COLS:]
        score = proj_words[:, 0:TB * 2 * D].rearrange("p (b r n) -> p b r n", b=TB, n=KEYS)
        cand_words = proj_words[:, 4 * D:6 * D]
        cand = cand_words.rearrange("p (h a b) -> p h a b", h=H, a=TOPK)
        onehot = cand_words.rearrange("p (m a) -> p m a", a=TOPK)
        routing = proj_words[:, 6 * D:]
        taken = [0]

        def route_part(words):
            taken[0] += words
            return routing[:, taken[0] - words:taken[0]]

        top1 = route_part(256).rearrange("p (r k) -> p r k", k=TOPK)
        top1_at = route_part(256).bitcast(U32).rearrange("p (r k) -> p r k", k=TOPK)
        top1_f = route_part(256).rearrange("p (r k) -> p r k", k=TOPK)
        top2 = route_part(TB * PAIRS).rearrange("p (b h k) -> p b h k", b=TB, k=TOPK)
        top2_at = route_part(TB * PAIRS).bitcast(U32).rearrange("p (b m) -> p b m", b=TB)
        digit = route_part(PAIRS).bitcast(U32)
        digit_f = route_part(PAIRS)
        routed = route_part(TB * 3 * PAIRS).rearrange("p (b w m) -> p b w m", b=TB, w=3)

        def quarter(slot, q):
            return w_slot[:, slot, 2 * q:2 * q + 2].rearrange("p k n -> p (k n)")

        bank = [ctx.enter_context(nc.psum_tensor(f"bank{n}", [P, COLS], F32)) for n in range(8)]
        y_bank = bank[0:4]
        z_bank = bank[0:2] + bank[4:6]
        ut_bank = bank[4:6]
        act_bank = bank[6:8]
        gate_bank = bank[0:4]

        def score_bank(b, m):
            return bank[(4 if b == 0 else 0) + m][:, :].rearrange("p (r n) -> p r n", n=KEYS)

        def signal(name, per_layer=0):
            return Signal(ctx, nc, name, per_layer)

        c_in = signal("c_in")
        inputs_in = signal("inputs_in")
        c_made = signal("c_made")
        masks_made = signal("masks_made")
        setup_transposed = signal("setup_transposed")
        setup_done = signal("setup_done")
        arena_free = signal("arena_free", 1)
        slots_free = signal("slots_free", 1)
        slot_in = [signal(f"slot_in{s}", 16 * N_WEIGHTS // 2) for s in range(2)]
        shift_in = [[signal(f"shift_in{s}{half}", 16 * N_SHIFT // 2) for half in range(2)] for s in range(2)]
        later_in = [signal(f"later_in{half}", 16 * N_LATER) for half in range(2)]
        ada_step = signal("ada_step", (K - 1) * N_ADA)
        ada_summed = signal("ada_summed", N_ADA)
        forget_w_in = signal("forget_w_in", 16)
        keys_in = signal("keys_in", 32)
        mod_summed = signal("mod_summed", N_ADA)
        mod_made = signal("mod_made", N_ADA)
        gain_made = signal("gain_made", 2)
        squares = signal("squares", 2 * TB)
        root_made = signal("root_made", 2)
        normed = signal("normed", 2 * TB)
        qk_mean = signal("qk_mean", 2 * TB)
        qk_root = signal("qk_root", 2 * TB)
        norm_transposed = signal("norm_transposed", 2 * 4)
        h_t_made = [signal(f"h_t_made{b}", 2 * K) for b in range(TB)]
        part_hi = signal("part_hi", 4 * N_WEIGHTS)
        part_lo = signal("part_lo", 4 * N_WEIGHTS)
        parts_used = signal("parts_used", 4 * N_WEIGHTS)
        proj_kept = signal("proj_kept", TB * N_PROJ)
        forget_summed = signal("forget_summed", 1)
        forget_abs = signal("forget_abs", 1)
        forget_log = signal("forget_log", 2)
        log_f_made = signal("log_f_made", 1)
        cum_f_summed = signal("cum_f_summed", 1)
        aug_made = signal("aug_made", 1)
        qk_turned = signal("qk_turned", H + H // 2)
        qk_kept = signal("qk_kept", H + H // 2)
        fox_scored = signal("fox_scored", H)
        fox_max = signal("fox_max", H)
        fox_exp = signal("fox_exp", 2 * H)
        fox_probs = signal("fox_probs", H)
        probs_turned = signal("probs_turned", H)
        probs_kept = signal("probs_kept", H)
        sb_scored = signal("sb_scored", H)
        sb_abs = signal("sb_abs", H)
        sb_log = signal("sb_log", 2 * H)
        sb_keep_made = signal("sb_keep_made", H)
        sb_summed = signal("sb_summed", H)
        sb_weights = signal("sb_weights", H)
        y_summed = signal("y_summed", H)
        y_hi_made = signal("y_hi_made", H)
        y_split = signal("y_split", H)
        gates_made = signal("gates_made", TB)
        merged_made = signal("merged_made", 4)
        merged_turned = signal("merged_turned", 4)
        merged_hi_made = signal("merged_hi_made", 4)
        merged_split = signal("merged_split", 4)
        diag_made = signal("diag_made", 2)
        row_summed = signal("row_summed", 2 * 2)
        row_kept = signal("row_kept", 2 * 2)
        x_mixed = signal("x_mixed", 4)
        h_hi_made = signal("h_hi_made", 2 * 4)
        h_lo_made = signal("h_lo_made", 2 * 4)
        pq_kept = signal("pq_kept", H)
        keys_turned = signal("keys_turned", 2)
        keys_kept = signal("keys_kept", 2)
        scored = signal("scored", 4 * TB)
        scores_kept = signal("scores_kept", 3 * TB)
        last_scores_kept = signal("last_scores_kept", TB)
        soft_sub = signal("soft_sub", TB)
        soft_exp = signal("soft_exp", 1)
        route_made = signal("route_made", 1)
        route_turned = signal("route_turned", TB)
        route_kept = signal("route_kept", TB)
        hot1_made = signal("hot1_made", N_GROUPS)
        hot2_made = signal("hot2_made", N_GROUPS)
        hot1_gated = signal("hot1_gated", N_GROUPS)
        gates_summed = signal("gates_summed", N_GROUPS)
        gates_kept = signal("gates_kept", N_GROUPS)
        gates_used = signal("gates_used", N_GROUPS)
        ones_laid = signal("ones_laid", 2)
        u_landed = [signal(f"u_landed{s}", 16 * BLOCKS // 2) for s in range(2)]
        v_landed = [signal(f"v_landed{s}", 16 * BLOCKS // 4) for s in range(4)]
        ut_turned = signal("ut_turned", 2 * BLOCKS)
        ut_hi_made = signal("ut_hi_made", 2 * BLOCKS)
        ut_lo_made = signal("ut_lo_made", 2 * BLOCKS)
        act_summed = signal("act_summed", BLOCKS)
        act_made = signal("act_made", BLOCKS)
        weight_made = signal("weight_made", BLOCKS - EARLY)
        w_hi_made = signal("w_hi_made", BLOCKS)
        w_split = signal("w_split", BLOCKS)
        v_hi_made = signal("v_hi_made", BLOCKS)
        v_split = signal("v_split", BLOCKS)
        y_added = signal("y_added", BLOCKS)
        x_done = signal("x_done", 4)
        stored = signal("stored")
        dve_step = signal("dve_step")

        BETWEEN = 1.45
        SETUP = 5
        MASKS = 19

        block = ctx.enter_context(nc.Block())

        @block.sync
        def _(sp):
            sp.dma_start(c_rows, c.rearrange("o (k p) -> (o k) p", p=P)).then_inc(c_in.sem, 16)
            ada_rows = ada_w.rearrange("l d n -> (l d) n")

            def ada_half(slot, half, arrived, of_layer, n):
                src = ada_rows[bass.ds(of_layer * D + half * D // 2, D // 2), n * COLS:(n + 1) * COLS]
                sp.dma_start(slots[slot][:, half * K // 2:(half + 1) * K // 2],
                             src.rearrange("(k p) n -> p k n", p=P)).then_inc(arrived.sem, 16)

            def shift_half(n, half, l, of_layer):
                if n >= 2 and half == 0:
                    sp.wait_ge(ada_step.sem, ada_step.by(l, (K - 1) * (n - 2) + K // 2))
                elif n >= 2:
                    sp.wait_ge(ada_summed.sem, ada_summed.by(l, n - 1))
                ada_half(n % 2, half, shift_in[n % 2][half], of_layer, n)

            for half in range(2):
                shift_half(0, half, 0, 0)
            sp.dma_start(x_sb[:, :, :], x.rearrange("o (b p) d -> p (o b) d", p=P)).then_inc(inputs_in.sem, 16)
            for l in range(L):
                at = l * PAR
                for rows, n in ((ada_b, 6 * K), (attn_norm, K), (ffn_norm, K)):
                    sp.dma_start(par_rows[at:at + n, :], rows[l, :].rearrange("(k p) -> k p", p=P))\
                        .then_inc(inputs_in.sem, 16)
                    at += n
                at = l * ROWC
                for rows, n in ((fox_q_gain, HD), (fox_k_gain, HD), (fox_bf, H)):
                    sp.dma_start(row_consts[:, at:at + n], rows[l:l + 1, :]).then_inc(inputs_in.sem, 16)
                    at += n
            for n in range(1, N_SHIFT):
                for half in range(2):
                    shift_half(n, half, 0, 0)

            with sp.Fori(0, L) as l:
                def slot_free(n):
                    if n < 2:
                        sp.wait_ge(ada_summed.sem, ada_summed.by(l, n + 3))
                    else:
                        sp.wait_ge(part_lo.sem, part_lo.by(l, 4 * (n - 1)))

                def weight_chunk(n, weight, col, wait=True):
                    if wait:
                        slot_free(n)
                    src = weight[bass.ds(l * D, D), col:col + COLS].rearrange("(k p) n -> p k n", p=P)
                    sp.dma_start(slots[n % 2], src).then_inc(slot_in[n % 2].sem, 16)

                in_rows = w_in.rearrange("l d n -> (l d) n")

                def ada_chunk(n):
                    for half in range(2):
                        if n == N_SHIFT:
                            sp.wait_ge(arena_free.sem, arena_free.by(l, 1))
                        elif half == 0:
                            sp.wait_ge(ada_step.sem, ada_step.by(l, (K - 1) * (n - 1) + K // 2))
                        else:
                            sp.wait_ge(ada_summed.sem, ada_summed.by(l, n))
                        ada_half(2, half, later_in[half], l, n)

                slot_free(0)
                sp.dma_start(forget_w, in_rows[bass.ds(l * D, D), FA:FA + H]
                             .rearrange("(k p) n -> p k n", p=P)).then_inc(forget_w_in.sem, 16)
                for n in range(N_PROJ):
                    weight_chunk(n, in_rows, n * COLS + (H if n * COLS >= FA else 0), wait=n > 0)
                    if 1 <= n <= N_LATER:
                        ada_chunk(N_SHIFT + n - 1)
                for n in range(N_BRANCH):
                    weight_chunk(AT_BRANCH + n, w_branch.rearrange("l g c n -> (l g c) n"), n * COLS)
                for n in range(N_OUT):
                    weight_chunk(AT_OUT + n, w_out.rearrange("l d n -> (l d) n"), n * COLS)
                for n, k_part in enumerate((peer_k1, peer_k2)):
                    sp.dma_start(keys[:, :, n * HD:(n + 1) * HD],
                                 k_part.rearrange("l h n d -> (l h) n d")[bass.ds(l * H, H)]
                                 .rearrange("h n d -> n h d")).then_inc(keys_in.sem, 16)
                for n in range(N_WQ):
                    weight_chunk(AT_WQ + n, peer_wq.rearrange("l d n -> (l d) n"), n * COLS)

                u_rows = peer_u.rearrange("l e d -> (l e) d")
                v_rows = peer_v.rearrange("l e d -> (l e) d")

                def expert_rows(landed, at, rows, n):
                    row = (l * BLOCKS + n) * KEYS
                    sp.dma_start(rows_in[:, at], rows[bass.ds(row, KEYS), :]).then_inc(landed.sem, 16)

                sp.wait_ge(ada_summed.sem, ada_summed.by(l, N_ADA))
                for s in range(2):
                    expert_rows(u_landed[s], s, u_rows, s)
                with sp.Fori(1, BLOCKS // 2) as i:
                    for s in range(2):
                        n = 2 * i + s
                        sp.wait_ge(ut_turned.sem, ut_turned.by(l, 2 * (n - 1)))
                        expert_rows(u_landed[s], s, u_rows, n)
                for n in range(4):
                    if n >= 2:
                        sp.wait_ge(ut_turned.sem, ut_turned.by(l, 2 * (BLOCKS + n - 3)))
                    expert_rows(v_landed[n], (n + 2) % 4, v_rows, n)

                def output_rows(n, s):
                    sp.wait_ge(v_split.sem, v_split.by(l, n - 3))
                    expert_rows(v_landed[s], (s + 2) % 4, v_rows, n)

                with sp.Fori(1, SHIFT_LOADS[0] // 4) as i:
                    for s in range(4):
                        output_rows(4 * i + s, s)
                sp.wait_ge(slots_free.sem, slots_free.by(l, 1))
                for n in range(SHIFT_LOADS[0], SHIFT_LOADS[-1] + 4):
                    for half in range(2):
                        if n - 2 * half in SHIFT_LOADS:
                            shift_half(SHIFT_LOADS.index(n - 2 * half), half, l + 1, (l + 1) % L)
                    output_rows(n, n % 4)
                with sp.Fori(SHIFT_LOADS[-1] // 4 + 1, BLOCKS // 4) as i:
                    for s in range(4):
                        output_rows(4 * i + s, s)
            sp.wait_ge(x_done.sem, L * 4)
            sp.dma_start(out.rearrange("o (b p) d -> p (o b) d", p=P), x_sb[:, :, :]).then_inc(stored.sem, 16)
            sp.wait_ge(stored.sem, 16)

        @block.gpsimd
        def _(pool):
            made = 0

            def mask(tile, value, fill, op, step, channel):
                nonlocal made
                nc.gpsimd.memset(tile, value).then_inc(masks_made.sem, 1)
                pool.wait_ge(masks_made.sem, made + 1)
                nc.gpsimd.affine_select(out=tile, in_=tile, compare_op=op, fill=fill, base=0,
                                        pattern=[[step, P]], channel_multiplier=channel)\
                    .then_inc(masks_made.sem, 1)
                made += 2

            mask(ident[:, :], 0.0, 1.0, ALU.not_equal, -1, 1)
            mask(cumsum_tri[:, :], 1.0, 0.0, ALU.is_ge, 1, -1)
            mask(neg_suffix_tri[:, :], -1.0, 0.0, ALU.is_ge, -1, 1)
            for at in (0, 2 * P):
                mask(mask_rows[:, 0, at:at + P], NEG, 0.0, ALU.is_gt, 1, -1)
                mask(mask_rows[:, 1, at:at + P], NEG, 0.0, ALU.is_ge, -1, 1)
            nc.gpsimd.memset(mask_rows[:, :, P:2 * P], 0.0).then_inc(masks_made.sem, 1)
            nc.gpsimd.memset(ones[:, :], 1.0).then_inc(masks_made.sem, 1)
            nc.gpsimd.memset(neg_ones[:, :], -1.0).then_inc(masks_made.sem, 1)
            nc.gpsimd.memset(eps[:, :], EPS).then_inc(masks_made.sem, 1)
            nc.gpsimd.iota(iota[:, :], [[1, P]], base=0, channel_multiplier=0,
                           allow_small_or_imprecise_dtypes=True).then_inc(masks_made.sem, 1)
            assert made + 5 == MASKS

            behind_proj = (T * KEYS - TB * N_PROJ * COLS) // T

            def lay_ones(first, after):
                to = arena[:, first * T:after * T]
                one = ones[:, 0:1].to_broadcast([P, (after - first) * T])
                nc.gpsimd.tensor_tensor(to, one, one, ALU.mult).then_inc(ones_laid.sem, 1)

            pool.wait_ge(masks_made.sem, MASKS)
            with pool.Fori(0, L) as l:
                with pool.Fori(0, N_WEIGHTS // 2) as i:
                    for slot in range(2):
                        for q in range(4):
                            pool.wait_ge(part_hi.sem, part_hi.by(l, 8 * i + 4 * slot + q + 1))
                            nc.gpsimd.tensor_tensor(rows_lo[:, q % 2], quarter(slot, q),
                                                    rows_hi[:, q % 2].bitcast(F32), ALU.subtract)\
                                .then_inc(part_lo.sem, 1)
                pool.wait_ge(scored.sem, scored.by(l, 4 * TB))
                lay_ones(EARLY, behind_proj)
                pool.wait_ge(soft_sub.sem, soft_sub.by(l, 1))
                lay_ones(behind_proj, LATE_AT)

        @block.scalar
        def _(sc):
            nc.scalar.preload_act_table(ACT.Silu)
            sc.wait_ge(setup_transposed.sem, 1)
            nc.scalar.activation(c_t[:, :], bank[1][:, 0:K], ACT.Silu).then_inc(c_made.sem, 1)
            sc.wait_ge(setup_transposed.sem, 3)
            nc.scalar.activation(par_t[:, :], bank[0][:, 0:P], ACT.Copy).then_inc(setup_done.sem, 1)
            nc.scalar.activation(rows_bc[:, :], bank[2][:, 0:L * ROWC], ACT.Copy).then_inc(setup_done.sem, 1)

            nc.scalar.activation(ident_r[:, :], ident[:, :], ACT.Copy).then_inc(setup_done.sem, 1)
            nc.scalar.activation(fox_mask[:, :], mask_rows[:, 0], ACT.Copy).then_inc(setup_done.sem, 1)
            nc.scalar.activation(sb_mask[:, :], mask_rows[:, 1], ACT.Copy).then_inc(setup_done.sem, 1)
            nc.scalar.preload_act_table(ACT.Sqrt)

            with sc.Fori(0, L) as l:
                def norm(which):
                    for b in range(TB):
                        if which == 0:
                            sc.wait_ge(arena_free.sem, arena_free.by(l, 1))
                        else:
                            sc.wait_ge(x_mixed.sem, x_mixed.by(l, 3 + b))
                        if b:
                            sc.wait_ge(squares.sem, squares.by(l, which * TB + b))
                        nc.scalar.activation(junk, x_sb[:, b], ACT.Square, scale=D ** -0.5,
                                             accum_out=stat[:, 0, b:b + 1])\
                            .then_inc(squares.sem, 1)
                    sc.wait_ge(squares.sem, squares.by(l, TB * (which + 1)))
                    nc.scalar.activation(stat[:, 1], stat[:, 0], ACT.Sqrt, bias=eps[:, :]).then_inc(root_made.sem, 1)
                    sc.wait_ge(gain_made.sem, gain_made.by(l, which + 1))
                    for k in range(K):
                        sc.wait_ge(norm_transposed.sem, norm_transposed.by(l, 4 * which + 1 + k // 4))
                        nc.scalar.activation(h_t[:, k, 0:P], bank[4 + k // 4][:, k % 4 * P:(k % 4 + 1) * P],
                                             ACT.Identity, scale=gain[:, which, k:k + 1],
                                             bias=mod[:, 3 * which * K + k:3 * which * K + k + 1])\
                            .then_inc(h_t_made[0].sem, 1)

                norm(0)

                def high_input(which):
                    for q in range(4):
                        for made in h_t_made:
                            sc.wait_ge(made.sem, made.by(l, K * which + 2 * q + 2))
                        nc.scalar.activation(h_hi[:, 2 * q:2 * q + 2], h_t[:, 2 * q:2 * q + 2], ACT.Copy)\
                            .then_inc(h_hi_made.sem, 1)

                def high_quarter(n, slot, before, q, first=False):
                    if q == 0:
                        sc.wait_ge(slot_in[slot].sem, slot_in[slot].by(l, 16 * (before + 1)))
                    if not first:
                        sc.wait_ge(parts_used.sem, parts_used.by(l, 4 * n + q - 1))
                    nc.scalar.activation(rows_hi[:, q % 2], quarter(slot, q), ACT.Copy).then_inc(part_hi.sem, 1)

                def high_quarters(n, quarters, **how):
                    for q in quarters:
                        high_quarter(n, n % 2, n // 2, q, **how)

                def keep_projection(n, s):
                    sc.wait_ge(parts_used.sem, parts_used.by(l, 4 * n + 4))
                    for b in range(TB):
                        at = slice(n * COLS, (n + 1) * COLS) if isinstance(n, int) else bass.ds(n * COLS, COLS)
                        nc.scalar.activation(proj[:, b, at], bank[2 * s + b][:, :], ACT.Copy)\
                            .then_inc(proj_kept.sem, 1)

                high_input(0)
                high_quarters(0, (0, 1), first=True)
                high_quarters(0, (2, 3))
                for n in range(1, 4):
                    high_quarters(n, (0, 1))
                    keep_projection(n - 1, (n - 1) % 2)
                    high_quarters(n, (2, 3))
                    if n == 2:
                        for m in range(2 * TB):
                            sc.wait_ge(qk_mean.sem, qk_mean.by(l, m + 1))
                            means = small[:, 64 + m * H:64 + (m + 1) * H]
                            nc.scalar.activation(means, means, ACT.Sqrt, bias=eps[:, :]).then_inc(qk_root.sem, 1)
                nc.scalar.preload_act_table_set("natural_log_exp_and_others")
                sc.wait_ge(forget_abs.sem, forget_abs.by(l, 1))
                nc.scalar.activation(small[:, 16:32], small[:, 16:32], ACT.Exp, scale=-1.0)\
                    .then_inc(forget_log.sem, 1)
                sc.wait_ge(forget_log.sem, forget_log.by(l, 1))
                nc.scalar.activation(small[:, 16:32], small[:, 16:32], ACT.Ln, bias=1.0)\
                    .then_inc(forget_log.sem, 1)
                with sc.Fori(2, N_PROJ // 2) as i:
                    for s in range(2):
                        n = 2 * i + s
                        for q in range(4):
                            high_quarter(n, s, i, q)
                            if q == 1:
                                keep_projection(n - 1, 1 - s)
                keep_projection(N_PROJ - 1, 1)

                def keep_qk(n):
                    sc.wait_ge(qk_turned.sem, qk_turned.by(l, n + 1))
                    src = bank[4 + n % 2]
                    if n < H:
                        nc.scalar.activation(fox_qk[0:AUG, n], src[0:AUG, :], ACT.Copy).then_inc(qk_kept.sem, 1)
                    else:
                        nc.scalar.activation(sb_qk[:, n - H, 0:T], src[:, 0:T], ACT.Copy, scale=HD ** -0.5)
                        nc.scalar.activation(sb_qk[:, n - H, T:2 * T], src[:, T:2 * T], ACT.Copy)\
                            .then_inc(qk_kept.sem, 1)

                def fox_exps(h):
                    sc.wait_ge(fox_max.sem, fox_max.by(l, h + 1))
                    if h >= 2:
                        sc.wait_ge(probs_turned.sem, probs_turned.by(l, h - 1))
                    for b, (at, n) in enumerate(((0, P), (P, 2 * P))):
                        nc.scalar.activation(probs[:, h % 2, at:at + n], bank[h % 2][:, at:at + n], ACT.Exp,
                                             bias=small[:, 40 + 2 * (h % 2) + b:41 + 2 * (h % 2) + b],
                                             accum_out=small[:, 48 + 2 * (h % 2) + b:49 + 2 * (h % 2) + b])\
                            .then_inc(fox_exp.sem, 1)

                def keep_probs(h):
                    sc.wait_ge(probs_turned.sem, probs_turned.by(l, h + 1))
                    if h >= 2 and h % 2 == 0:
                        sc.wait_ge(y_summed.sem, y_summed.by(l, h // 2))
                    nc.scalar.activation(probs_t[:, h % 2], bank[2 + h % 2][:, 0:CAUSAL], ACT.Copy)\
                        .then_inc(probs_kept.sem, 1)

                def high_y(n):
                    sc.wait_ge(y_summed.sem, y_summed.by(l, n + 1))
                    nc.scalar.activation(h_hi[:, n], bank[6 + n % 2][:, 0:T], ACT.Copy).then_inc(y_hi_made.sem, 1)

                keep_qk(0)
                keep_qk(1)
                for h in range(H + 2):
                    if h < H:
                        fox_exps(h)
                    if h + 2 < H:
                        keep_qk(h + 2)
                    if h >= 2:
                        keep_probs(h - 2)
                    if h >= 4 and h % 2 == 0:
                        high_y(h // 2 - 2)
                high_y(H // 2 - 1)
                for n in range(H, H + H // 2):
                    keep_qk(n)
                high_quarters(AT_BRANCH, (0, 1))

                def softplus_tail(h):
                    s = h % 2
                    sc.wait_ge(sb_scored.sem, sb_scored.by(l, h + 1))
                    if h >= 2:
                        sc.wait_ge(sb_keep_made.sem, sb_keep_made.by(l, h - 1))
                    nc.scalar.activation(soft[:, s], z_bank[h % 4][:, 0:CAUSAL], ACT.Abs).then_inc(sb_abs.sem, 1)
                    sc.wait_ge(sb_abs.sem, sb_abs.by(l, h + 1))
                    nc.scalar.activation(soft[:, s], soft[:, s], ACT.Exp, scale=-1.0).then_inc(sb_log.sem, 1)
                    sc.wait_ge(sb_log.sem, sb_log.by(l, 2 * h + 1))
                    nc.scalar.activation(soft[:, s], soft[:, s], ACT.Ln, bias=1.0).then_inc(sb_log.sem, 1)

                def sb_exp(h):
                    sc.wait_ge(sb_summed.sem, sb_summed.by(l, h + 1))
                    if h % 2 == 0:
                        sc.wait_ge(y_summed.sem, y_summed.by(l, H // 2 + h // 2))
                    nc.scalar.activation(probs_t[:, h % 2], bank[2 + h % 2][:, 0:CAUSAL], ACT.Exp)\
                        .then_inc(sb_weights.sem, 1)

                for h in range(H + 1):
                    if h < H:
                        softplus_tail(h)
                    if h >= 1:
                        sb_exp(h - 1)
                        if h % 2 == 0:
                            high_y(H // 2 + h // 2 - 1)
                for b in range(TB):
                    nc.scalar.activation(gates[:, b], gates[:, b], ACT.Sigmoid).then_inc(gates_made.sem, 1)
                def keep_row(which):
                    for n in range(2):
                        src = bank[n if which == 0 else 4 + n]
                        sc.wait_ge(row_summed.sem, row_summed.by(l, 2 * which + n + 1))
                        nc.scalar.activation(gate_row[:, n * COLS:(n + 1) * COLS], src[:, :], ACT.Copy)\
                            .then_inc(row_kept.sem, 1)

                high_quarters(AT_BRANCH, (2, 3))
                high_quarters(AT_BRANCH + 1, range(4))
                high_quarters(AT_OUT, (0, 1))
                for n in range(4):
                    sc.wait_ge(merged_turned.sem, merged_turned.by(l, n + 1))
                    dst = h_hi[:, 4 * (n % 2):4 * (n % 2) + 4, n // 2 * P:(n // 2 + 1) * P]
                    nc.scalar.activation(dst, bank[4 + n][:, :].rearrange("p (k t) -> p k t", k=4), ACT.Copy)\
                        .then_inc(merged_hi_made.sem, 1)
                high_quarters(AT_OUT, (2, 3))
                high_quarters(AT_OUT + 1, (0, 1))
                keep_row(0)
                nc.scalar.preload_act_table(ACT.Sqrt)
                high_quarters(AT_OUT + 1, (2, 3))
                high_quarters(AT_WQ, (0, 1))
                norm(1)
                high_input(1)

                def keep_queries(n):
                    sc.wait_ge(parts_used.sem, parts_used.by(l, 4 * (AT_WQ + n) + 4))
                    for h in range(4 * n, 4 * n + 4):
                        nc.scalar.activation(pq_t[:, h], bank[h][:, 0:T], ACT.Copy).then_inc(pq_kept.sem, 1)

                high_quarters(AT_WQ, (2, 3))
                high_quarters(AT_WQ + 1, (0, 1))
                keep_queries(0)
                high_quarters(AT_WQ + 1, (2, 3))
                keep_queries(1)
                for n in range(2):
                    sc.wait_ge(keys_turned.sem, keys_turned.by(l, n + 1))
                    nc.scalar.activation(keys_t[:, 4 * n:4 * n + 4],
                                         bank[2 + n][:, :].rearrange("p (h n) -> p h n", n=P), ACT.Copy)\
                        .then_inc(keys_kept.sem, 1)
                for b in range(TB):
                    for n in range(3):
                        m = 2 * (n % 2) + n // 2
                        sc.wait_ge(scored.sem, scored.by(l, 4 * b + n + 1))
                        nc.scalar.activation(score[:, b, 4 * m:4 * m + 4], score_bank(b, m), ACT.Copy)\
                            .then_inc(scores_kept.sem, 1)

                nc.scalar.preload_act_table(ACT.Gelu)

                def ut_high(n, s, wait=True):
                    if wait:
                        sc.wait_ge(act_summed.sem, act_summed.by(l, n - 1))
                    for half in range(2):
                        sc.wait_ge(ut_turned.sem, ut_turned.by(l, 2 * n + half + 1))
                        nc.scalar.activation(rows_hi[:, s, half * COLS:(half + 1) * COLS], ut_bank[half][:, :],
                                             ACT.Copy).then_inc(ut_hi_made.sem, 1)

                def gelu_early(n, s):
                    sc.wait_ge(act_summed.sem, act_summed.by(l, n + 1))
                    at = n if isinstance(n, int) else bass.ds(n, 1)
                    out = weight[:, at] if isinstance(n, int) else weight[:, at].squeeze(1)
                    nc.scalar.activation(out, act_bank[s][:, 0:T], ACT.Gelu).then_inc(act_made.sem, 1)

                def gelu(n, s):
                    sc.wait_ge(act_summed.sem, act_summed.by(l, n + 1))
                    if not isinstance(n, int) or n >= EARLY + 2:
                        sc.wait_ge(weight_made.sem, weight_made.by(l, n - EARLY - 1))
                    nc.scalar.activation(act[:, s], act_bank[s][:, 0:T], ACT.Gelu).then_inc(act_made.sem, 1)

                ut_high(0, 0, wait=False)
                ut_high(1, 1, wait=False)
                gelu_early(0, 0)
                ut_high(2, 0)
                gelu_early(1, 1)

                def early_blocks(first, after):
                    with sc.Fori(first // 2, after // 2) as i:
                        for s in range(2):
                            ut_high(2 * i + s + 1, 1 - s)
                            gelu_early(2 * i + s, s)

                early_blocks(2, ROUTED - 2)
                sc.wait_ge(soft_sub.sem, soft_sub.by(l, TB))
                nc.scalar.activation(top2, top2, ACT.Exp).then_inc(soft_exp.sem, 1)
                for s in range(2):
                    ut_high(ROUTED - 2 + s + 1, 1 - s)
                    gelu_early(ROUTED - 2 + s, s)
                for b in range(TB):
                    sc.wait_ge(route_turned.sem, route_turned.by(l, b + 1))
                    nc.scalar.activation(route_t[:, :, b * P:(b + 1) * P],
                                         bank[b][:, 0:3 * P].rearrange("p (w t) -> p w t", w=3), ACT.Copy)\
                        .then_inc(route_kept.sem, 1)
                def gate_hots(g, s):
                    sc.wait_ge(hot1_made.sem, hot1_made.by(l, g + 1))
                    for t in range(GROUP):
                        at = g * GROUP + t
                        at = slice(at, at + 1) if isinstance(g, int) else bass.ds(at, 1)
                        ins = nc.scalar.activation(hot1[:, s * GROUP + t], hot1[:, s * GROUP + t], ACT.Copy,
                                                   scale=route_t[:, 2, at])
                    ins.then_inc(hot1_gated.sem, 1)

                for g in range(2):
                    gate_hots(g, g)
                early_blocks(ROUTED, EARLY)

                def keep_gates(g, j):
                    sc.wait_ge(gates_summed.sem, gates_summed.by(l, g + 1))
                    of = gate_bank[j][:, :].rearrange("p (t e) -> p t e", t=GROUP)
                    at = slice(g * GROUP, (g + 1) * GROUP) if isinstance(g, int) else bass.ds(g * GROUP, GROUP)
                    nc.scalar.activation(weight[:, LATE_AT:, at].rearrange("p e t -> p t e"), of[:, :, LATE_AT:],
                                         ACT.Copy).then_inc(gates_kept.sem, 1)

                def gates_and_block(i, m, last=False):
                    for j in (2 * m, 2 * m + 1):
                        keep_gates(4 * i + j, j)
                    ut_high(EARLY + 2 * i + m + 1, 1 - m)
                    if not last:
                        for j in (2 * m, 2 * m + 1):
                            gate_hots(4 * i + j + 2, j % 2)
                    gelu(EARLY + 2 * i + m, m)

                for m in range(2):
                    gates_and_block(0, m)
                with sc.Fori(1, MIDDLE // 2 - 1) as i:
                    for m in range(2):
                        gates_and_block(i, m)
                gates_and_block(MIDDLE // 2 - 1, 0)
                gates_and_block(MIDDLE // 2 - 1, 1, last=True)
                with sc.Fori(LATE_AT // 2, BLOCKS // 2 - 1) as i:
                    for s in range(2):
                        ut_high(2 * i + s + 1, 1 - s)
                        gelu(2 * i + s, s)
                ut_high(BLOCKS - 1, 1)
                gelu(BLOCKS - 2, 0)
                gelu(BLOCKS - 1, 1)

                def v_high(n, s, i):
                    sc.wait_ge(v_landed[s].sem, v_landed[s].by(l, 16 * i + 16))
                    if not isinstance(n, int) or n >= 2:
                        sc.wait_ge(y_added.sem, y_added.by(l, n - 1))
                    nc.scalar.activation(rows_hi[:, s % 2], rows_in[:, (s + 2) % 4], ACT.Copy)\
                        .then_inc(v_hi_made.sem, 1)

                for s in range(4):
                    v_high(s, s, 0)
                rows_at = ROWS_AT // 4 + 2
                with sc.Fori(1, rows_at) as i:
                    for s in range(4):
                        v_high(4 * i + s, s, i)
                keep_row(1)
                with sc.Fori(rows_at, BLOCKS // 4) as i:
                    for s in range(4):
                        v_high(4 * i + s, s, i)
                nc.scalar.preload_act_table(ACT.Sqrt)

        @block.vector
        def _(ve):
            def ada_product(l, n, s):
                first = isinstance(n, int) and n < N_SHIFT
                slot, arrived, before = (s, shift_in[s], n // 2) if first else (2, later_in, n - N_SHIFT)
                if not isinstance(n, int) or n >= 2:
                    ve.wait_ge(mod_summed.sem, mod_summed.by(l, n - 1))
                for k in range(K):
                    if k % (K // 2) == 0:
                        half = arrived[k // (K // 2)]
                        ve.wait_ge(half.sem, half.by(l, 16 * (before + 1)))
                    if k == 0:
                        ins = V.tensor_scalar(ada_sum[:, s], slots[slot][:, 0], c_t[:, 0:1], None, ALU.mult)
                    else:
                        ve.wait_ge(ada_step.sem, ada_step.by(l, (K - 1) * n + k))
                        ins = V.scalar_tensor_tensor(ada_sum[:, s], slots[slot][:, k], c_t[:, k:k + 1],
                                                     ada_sum[:, s], ALU.mult, ALU.add)
                    ins.then_inc((ada_step if k < K - 1 else ada_summed).sem, 1)
                    yield k

            def modulation(l, n, to, of_layer):
                ve.wait_ge(mod_summed.sem, mod_summed.by(l, n + 1))
                cols = 4 * n
                at = slice(cols, cols + 4) if isinstance(n, int) else bass.ds(cols, 4)
                bias = of_layer * PAR + cols
                bias = slice(bias, bias + 4) if isinstance(bias, int) else bass.ds(bias, 4)
                V.tensor_tensor(mod[:, at], to[:, 0:4], par_t[:, bias], ALU.add).then_inc(mod_made.sem, 1)

            V = nc.vector
            ve.wait_ge(c_made.sem, 1)
            for n in range(N_SHIFT):
                for _ in ada_product(0, n, n % 2):
                    pass
            ve.wait_ge(setup_done.sem, SETUP)
            for n in range(N_SHIFT):
                modulation(0, n, bank[4 + n], 0)

            with ve.Fori(0, L) as l:
                steps = [0]
                ve.sem_clear(dve_step.sem)

                def mark(ins):
                    ins.then_inc(dve_step.sem, 1)
                    steps[0] += 1
                    return steps[0]

                def after(n):
                    ve.wait_ge(dve_step.sem, n)

                def link(ins):
                    after(mark(ins))

                def norm_gain(which):
                    ve.wait_ge(mod_made.sem, mod_made.by(l, N_ADA if which else N_SHIFT))
                    V.scalar_tensor_tensor(gain[:, which], mod[:, (3 * which + 1) * K:(3 * which + 2) * K], 1.0,
                                           par_t[:, bass.ds(l * PAR + (6 + which) * K, K)], ALU.add, ALU.mult)\
                        .then_inc(gain_made.sem, 1)

                def low_input(which, q):
                    ve.wait_ge(h_t_made[1].sem, h_t_made[1].by(l, K * which + 2 * q + 2))
                    ve.wait_ge(h_hi_made.sem, h_hi_made.by(l, 4 * which + q + 1))
                    at = slice(2 * q, 2 * q + 2)
                    V.tensor_tensor(h_lo[:, at], h_t[:, at], h_hi[:, at].bitcast(F32), ALU.subtract)\
                        .then_inc(h_lo_made.sem, 1)

                def norm(which):
                    ve.wait_ge(root_made.sem, root_made.by(l, which + 1))
                    link(V.reciprocal(stat[:, 1], stat[:, 1]))
                    for b in range(TB):
                        V.tensor_scalar(x_norm[:, b], x_sb[:, b], stat[:, 1, b:b + 1], None, ALU.mult)\
                            .then_inc(normed.sem, 1)
                    norm_gain(which)
                    ve.wait_ge(gain_made.sem, gain_made.by(l, which + 1))
                    for k in range(K):
                        ve.wait_ge(norm_transposed.sem, norm_transposed.by(l, 4 * which + 3 + k // 4))
                        V.tensor_scalar(h_t[:, k, P:T], bank[6 + k // 4][:, k % 4 * P:(k % 4 + 1) * P],
                                        gain[:, which, k:k + 1],
                                        mod[:, 3 * which * K + k:3 * which * K + k + 1], ALU.mult, ALU.add)\
                            .then_inc(h_t_made[1].sem, 1)
                        if k == K - 3:
                            low_input(which, 0)
                    for q in range(1, 4):
                        low_input(which, q)

                norm(0)
                link(V.memset(aug[:, 0, :, :, HD + 1], 1.0))
                link(V.memset(aug[:, 1, :, :, HD], 1.0))
                ve.wait_ge(forget_summed.sem, forget_summed.by(l, 1))
                for b in range(TB):
                    mark(V.tensor_tensor(small[:, b * H:(b + 1) * H], bank[4][:, b * H:(b + 1) * H],
                                         rows_bc[:, bass.ds(l * ROWC + 2 * HD, H)], ALU.add))
                after(steps[0])
                V.scalar_tensor_tensor(small[:, 16:32], small[:, 0:16], -1.0, small[:, 0:16], ALU.mult, ALU.max)\
                    .then_inc(forget_abs.sem, 1)

                parts = [(which, b, 64 + (TB * which + b) * H) for which in range(2) for b in range(TB)]
                for n in range(2):
                    for _ in ada_product(l, N_SHIFT + n, n):
                        pass
                for n, (which, b, at) in enumerate(parts):
                    src = proj[:, b, which * COLS:(which + 1) * COLS].rearrange("p (h n) -> p h n", h=H)
                    ve.wait_ge(proj_kept.sem, proj_kept.by(l, n + 1))
                    link(V.scalar_tensor_tensor(sq_junk, src, 1.0 / HD, src, ALU.mult, ALU.mult))
                    V.tensor_reduce(small[:, at:at + H], sq_junk, AX.X, ALU.add).then_inc(qk_mean.sem, 1)
                    ve.wait_ge(qk_mean.sem, qk_mean.by(l, n + 1))
                modulation(l, N_SHIFT, bank[6], l)
                for n, (which, b, at) in enumerate(parts):
                    src = proj[:, b, which * COLS:(which + 1) * COLS].rearrange("p (h n) -> p h n", h=H)
                    ve.wait_ge(qk_root.sem, qk_root.by(l, n + 1))
                    link(V.reciprocal(small[:, at:at + H], small[:, at:at + H]))
                    link(V.scalar_tensor_tensor(src, src, HD ** -0.5 if which == 0 else 1.0,
                                                small[:, at:at + H].unsqueeze(2).to_broadcast([P, H, HD]),
                                                ALU.mult, ALU.mult))
                    link(V.tensor_tensor(aug[:, which, b, :, 0:HD], src,
                                         rows_bc[:, bass.ds(l * ROWC + which * HD, HD)].unsqueeze(1)
                                         .to_broadcast([P, H, HD]), ALU.mult))
                with ve.Fori(N_SHIFT // 2 + 1, N_ADA // 2) as i:
                    for s in range(2):
                        for _ in ada_product(l, 2 * i + s, s):
                            pass
                        modulation(l, 2 * i + s - 1, bank[7 - s], l)
                modulation(l, N_ADA - 1, bank[7], l)
                ve.wait_ge(forget_log.sem, forget_log.by(l, 2))
                V.scalar_tensor_tensor(small[:, 0:16], small[:, 0:16], 0.0, small[:, 16:32],
                                       ALU.min, ALU.subtract).then_inc(log_f_made.sem, 1)

                ve.wait_ge(cum_f_summed.sem, cum_f_summed.by(l, 1))
                cum_f = bank[5][:, 0:TB * H].rearrange("p (b h) -> p b h", h=H)
                link(V.tensor_copy(aug[:, 0, :, :, HD], cum_f))
                V.tensor_scalar(aug[:, 1, :, :, HD + 1], cum_f, -1.0, None, ALU.mult).then_inc(aug_made.sem, 1)

                def fox_maxima(h):
                    ve.wait_ge(fox_scored.sem, fox_scored.by(l, h + 1))
                    if h >= 2:
                        ve.wait_ge(fox_exp.sem, fox_exp.by(l, 2 * (h - 1)))
                    o = 40 + 2 * (h % 2)
                    mark(V.tensor_reduce(small[:, o:o + 1], bank[h % 2][:, 0:P], AX.X, ALU.max, negate=True))
                    V.tensor_reduce(small[:, o + 1:o + 2], bank[h % 2][:, P:CAUSAL], AX.X, ALU.max, negate=True)\
                        .then_inc(fox_max.sem, 1)

                def fox_normalise(h):
                    s = h % 2
                    ve.wait_ge(fox_exp.sem, fox_exp.by(l, 2 * h + 2))
                    link(V.reciprocal(small[:, 52 + 2 * s:54 + 2 * s], small[:, 48 + 2 * s:50 + 2 * s]))
                    mark(V.tensor_scalar(probs[:, s, 0:P], probs[:, s, 0:P], small[:, 52 + 2 * s:53 + 2 * s],
                                         None, ALU.mult))
                    V.tensor_scalar(probs[:, s, P:CAUSAL], probs[:, s, P:CAUSAL],
                                    small[:, 53 + 2 * s:54 + 2 * s], None, ALU.mult).then_inc(fox_probs.sem, 1)

                def low_y(n):
                    ve.wait_ge(y_hi_made.sem, y_hi_made.by(l, n + 1))
                    V.tensor_tensor(h_lo[:, n], bank[6 + n % 2][:, 0:T], h_hi[:, n].bitcast(F32), ALU.subtract)\
                        .then_inc(y_split.sem, 1)

                for h in range(H + 1):
                    if h >= 6 and h % 2 == 0:
                        low_y(h // 2 - 3)
                    if h < H:
                        fox_maxima(h)
                    if h >= 1:
                        fox_normalise(h - 1)

                def sb_softplus(h):
                    s = h % 2
                    ve.wait_ge(sb_log.sem, sb_log.by(l, 2 * h + 2))
                    if h >= 2:
                        ve.wait_ge(sb_summed.sem, sb_summed.by(l, h - 1))
                    V.scalar_tensor_tensor(log_keep[:, s], z_bank[h % 4][:, 0:CAUSAL], 0.0, soft[:, s],
                                           ALU.max, ALU.add).then_inc(sb_keep_made.sem, 1)

                low_y(H // 2 - 2)
                low_y(H // 2 - 1)
                for h in range(H):
                    if h >= 4 and h % 2 == 0:
                        low_y(H // 2 + h // 2 - 2)
                    sb_softplus(h)
                low_y(H - 2)
                low_y(H - 1)

                for n in range(2):
                    for b in range(TB):
                        q = 2 * n + b
                        cols = slice(n * COLS, (n + 1) * COLS)
                        other = tmp[:, (q % 2) * COLS:(q % 2 + 1) * COLS]
                        ve.wait_ge(gates_made.sem, gates_made.by(l, b + 1))
                        ve.wait_ge(parts_used.sem, parts_used.by(l, 4 * (AT_BRANCH + n) + 4))
                        mark(V.tensor_tensor(merged[:, b, cols], bank[2 * q][:, :], gates[:, b, cols],
                                             ALU.mult))
                        link(V.tensor_tensor(other, bank[2 * q + 1][:, :],
                                             gates[:, b, D + n * COLS:D + (n + 1) * COLS], ALU.mult))
                        V.tensor_tensor(merged[:, b, cols], merged[:, b, cols], other, ALU.add)\
                            .then_inc(merged_made.sem, 1)

                for n in range(4):
                    at = slice(4 * (n % 2), 4 * (n % 2) + 4), slice(n // 2 * P, (n // 2 + 1) * P)
                    ve.wait_ge(merged_hi_made.sem, merged_hi_made.by(l, n + 1))
                    V.tensor_tensor(h_lo[:, at[0], at[1]], bank[4 + n][:, :].rearrange("p (k t) -> p k t", k=4),
                                    h_hi[:, at[0], at[1]].bitcast(F32), ALU.subtract).then_inc(merged_split.sem, 1)
                ve.wait_ge(mod_made.sem, mod_made.by(l, N_ADA))

                def diagonals(which):
                    for k in range(K):
                        g = (3 * which + 2) * K + k
                        ins = V.tensor_scalar(diag[:, k], ident[:, :], mod[:, g:g + 1], None, ALU.mult)
                        if k < K - 1:
                            mark(ins)
                        else:
                            ins.then_inc(diag_made.sem, 1)

                diagonals(0)
                ve.wait_ge(row_kept.sem, row_kept.by(l, 2))
                for n in range(2):
                    for b in range(TB):
                        q = 2 * n + b
                        cols = slice(n * COLS, (n + 1) * COLS)
                        mixed = tmp[:, (q % 2) * COLS:(q % 2 + 1) * COLS]
                        ve.wait_ge(parts_used.sem, parts_used.by(l, 4 * (AT_OUT + n) + 4))
                        link(V.tensor_tensor(mixed, bank[2 + 2 * n + b][:, :], gate_row[:, cols], ALU.mult))
                        V.tensor_tensor(x_sb[:, b, cols], x_sb[:, b, cols], mixed, ALU.add).then_inc(x_mixed.sem, 1)

                ve.wait_ge(x_mixed.sem, x_mixed.by(l, 4))
                norm(1)

                def top16(rows, top, at):
                    n = len(rows)
                    cost = 0.06 + rows[0].shape[1] / 960
                    first = steps[0]
                    for r in range(n):
                        mark(V.max(top[:, r, 0:8], rows[r]))
                        yield cost
                    for r in range(n):
                        after(first + r + 1)
                        mark(V.max_index(at[:, r, 0:8], top[:, r, 0:8], rows[r]))
                        yield cost
                    for r in range(n):
                        after(first + n + r + 1)
                        mark(V.match_replace(rows[r], top[:, r, 0:8], rows[r], LOWEST))
                        yield cost
                    for r in range(n):
                        after(first + 2 * n + r + 1)
                        mark(V.max(top[:, r, 8:16], rows[r]))
                        yield cost
                    for r in range(n):
                        after(first + 3 * n + r + 1)
                        mark(V.max_index(at[:, r, 8:16], top[:, r, 8:16], rows[r]))
                        yield cost
                    after(steps[0])

                def route(b):
                    ve.wait_ge(scores_kept.sem, scores_kept.by(l, 3 * (b + 1)))
                    ve.wait_ge(scored.sem, scored.by(l, 4 * (b + 1)))
                    V.tensor_copy(score[:, b, 12:16], score_bank(b, 3)).then_inc(last_scores_kept.sem, 1)
                    link(V.memset(small[:, 0:1], 0.0))
                    yield 0.7
                    yield from top16([score[:, b, r] for r in range(2 * H)], top1, top1_at)
                    mark(V.tensor_copy(top1_f, top1_at))
                    both = top1.rearrange("p (w h) k -> p h w k", w=2)
                    for h in range(H):
                        mark(V.tensor_tensor(cand[:, h], both[:, h, 0].unsqueeze(2).to_broadcast([P, TOPK, TOPK]),
                                             both[:, h, 1].unsqueeze(1).to_broadcast([P, TOPK, TOPK]), ALU.add))
                        yield 0.33
                    after(steps[0])
                    yield from top16([cand_words[:, h * 256:(h + 1) * 256] for h in range(H)], top2[:, b],
                                     top2_at[:, b].rearrange("p (h k) -> p h k", k=TOPK))
                    link(V.tensor_reduce(small[:, 0:H], top2[:, b], AX.X, ALU.max))
                    V.tensor_tensor(top2[:, b], top2[:, b], small[:, 0:H].unsqueeze(2).to_broadcast([P, H, TOPK]),
                                    ALU.subtract).then_inc(soft_sub.sem, 1)
                    ve.wait_ge(soft_sub.sem, soft_sub.by(l, b + 1))
                    yield 0.4
                    which_f = top1_f.rearrange("p (w h) k -> p h w k", w=2)
                    for w in range(2):
                        if w == 0:
                            link(V.tensor_single_scalar(digit, top2_at[:, b], 4, ALU.logical_shift_right))
                        else:
                            link(V.tensor_single_scalar(digit, top2_at[:, b], TOPK - 1, ALU.bitwise_and))
                        link(V.tensor_copy(digit_f, digit))
                        yield 0.3
                        link(V.tensor_tensor(onehot, digit_f.unsqueeze(2).to_broadcast([P, PAIRS, TOPK]),
                                             iota[:, 0:TOPK].unsqueeze(1).to_broadcast([P, PAIRS, TOPK]),
                                             ALU.is_equal))
                        yield 2.2
                        for h in range(H):
                            one = onehot[:, h * TOPK:(h + 1) * TOPK]
                            mark(V.tensor_tensor(one, one, which_f[:, h, w].unsqueeze(1)
                                                 .to_broadcast([P, TOPK, TOPK]), ALU.mult))
                            yield 0.33
                        after(steps[0])
                        link(V.tensor_reduce(routed[:, b, 1 - w], onehot, AX.X, ALU.add))
                        yield 2.2

                def ut_low(n, s, wait=True):
                    if wait:
                        ve.wait_ge(act_summed.sem, act_summed.by(l, n - 1))
                    for half in range(2):
                        cols = slice(half * COLS, (half + 1) * COLS)
                        ve.wait_ge(ut_hi_made.sem, ut_hi_made.by(l, 2 * n + half + 1))
                        V.tensor_tensor(rows_lo[:, s, cols], ut_bank[half][:, :], rows_hi[:, s, cols].bitcast(F32),
                                        ALU.subtract).then_inc(ut_lo_made.sem, 1)

                split, spent = 0, 0.0
                for b in range(TB):
                    for cost in route(b):
                        spent += cost
                        if spent > BETWEEN and split < ROUTED - 1:
                            ut_low(split, split % 2, wait=split >= 2)
                            split, spent = split + 1, 0.0
                for n in range(split, ROUTED - 1):
                    ut_low(n, n % 2)
                ve.wait_ge(soft_exp.sem, soft_exp.by(l, 1))
                for b in range(TB):
                    link(V.tensor_reduce(small[:, 8:8 + H], top2[:, b], AX.X, ALU.add))
                    link(V.reciprocal(small[:, 16:16 + H], small[:, 8:8 + H]))
                    ins = V.tensor_tensor(routed[:, b, 2].rearrange("p (h k) -> p h k", k=TOPK), top2[:, b],
                                          small[:, 16:16 + H].unsqueeze(2).to_broadcast([P, H, TOPK]), ALU.mult)
                    if b == 0:
                        link(ins)
                    else:
                        ins.then_inc(route_made.sem, 1)

                def one_hots(g, s, first=False):
                    if first:
                        ve.wait_ge(route_kept.sem, route_kept.by(l, TB))
                    else:
                        ve.wait_ge(gates_summed.sem, gates_summed.by(l, g - 1))
                    at = slice(g * GROUP, (g + 1) * GROUP) if first else bass.ds(g * GROUP, GROUP)
                    for which, hot in ((1, hot1), (0, hot2)):
                        V.tensor_tensor(hot[:, s * GROUP:(s + 1) * GROUP],
                                        iota[:, :].unsqueeze(1).to_broadcast([P, GROUP, P]),
                                        route_t[:, which, at].unsqueeze(2).to_broadcast([P, GROUP, P]),
                                        ALU.is_equal).then_inc((hot1_made if which else hot2_made).sem, 1)

                for n in range(ROUTED - 1, ROUTED + 1):
                    ut_low(n, n % 2)
                for s in range(2):
                    one_hots(s, s, True)
                for n in range(ROUTED + 1, EARLY + 1):
                    ut_low(n, n % 2)

                def gate_blocks(g, j):
                    ve.wait_ge(gates_kept.sem, gates_kept.by(l, g + 1))
                    at = slice(g * GROUP, (g + 1) * GROUP) if isinstance(g, int) else bass.ds(g * GROUP, GROUP)
                    to = weight[:, 0:LATE_AT, at].rearrange("p e t -> p t e")
                    V.tensor_tensor(to, to, gate_bank[j][:, :].rearrange("p (t e) -> p t e", t=GROUP)[:, :, 0:LATE_AT],
                                    ALU.mult).then_inc(gates_used.sem, 1)

                def weigh(n, s):
                    ve.wait_ge(act_made.sem, act_made.by(l, n + 1))
                    to = weight[:, n] if isinstance(n, int) else weight[:, bass.ds(n, 1)].squeeze(1)
                    V.tensor_tensor(to, to, act[:, s], ALU.mult).then_inc(weight_made.sem, 1)

                def gates_and_block(i, m, first=False, last=False):
                    n = EARLY + 2 * i + m
                    for j in (2 * m, 2 * m + 1):
                        g = 4 * i + j
                        if not last:
                            one_hots(g + 2, j % 2)
                        if not first and not (isinstance(i, int) and i == 0 and m == 1):
                            ve.wait_ge(weight_made.sem, weight_made.by(l, n - 1 - EARLY))
                        gate_blocks(g, j)
                    ut_low(n + 1, 1 - m)
                    if not first:
                        ve.wait_ge(gates_used.sem, gates_used.by(l, 4 * i + 2 * m + 2))
                        weigh(n - 1, 1 - m)

                ve.wait_ge(act_made.sem, act_made.by(l, EARLY))
                ve.wait_ge(ones_laid.sem, ones_laid.by(l, 2))
                gates_and_block(0, 0, first=True)
                gates_and_block(0, 1)
                with ve.Fori(1, MIDDLE // 2 - 1) as i:
                    for m in range(2):
                        gates_and_block(i, m)
                gates_and_block(MIDDLE // 2 - 1, 0)
                gates_and_block(MIDDLE // 2 - 1, 1, last=True)
                ve.wait_ge(gates_used.sem, gates_used.by(l, N_GROUPS))
                weigh(LATE_AT - 1, 1)
                ve.wait_ge(gates_kept.sem, gates_kept.by(l, N_GROUPS))
                ut_low(LATE_AT + 1, 1)
                with ve.Fori(LATE_AT // 2, BLOCKS // 2 - 1) as i:
                    for s in range(2):
                        weigh(2 * i + s, s)
                        ut_low(2 * i + s + 2, s)
                for s in range(2):
                    weigh(BLOCKS - 2 + s, s)

                def split_weights(n, s4):
                    s = s4 % 2
                    if not isinstance(n, int) or n >= 2:
                        ve.wait_ge(y_added.sem, y_added.by(l, n - 1))
                    of = weight[:, n] if isinstance(n, int) else weight[:, bass.ds(n, 1)].squeeze(1)
                    V.tensor_copy(w_hi[:, s], of).then_inc(w_hi_made.sem, 1)
                    ve.wait_ge(w_hi_made.sem, w_hi_made.by(l, n + 1))
                    V.tensor_tensor(w_lo[:, s], of, w_hi[:, s].bitcast(F32), ALU.subtract).then_inc(w_split.sem, 1)
                    ve.wait_ge(v_hi_made.sem, v_hi_made.by(l, n + 1))
                    V.tensor_tensor(rows_lo[:, s], rows_in[:, (s4 + 2) % 4], rows_hi[:, s].bitcast(F32),
                                    ALU.subtract).then_inc(v_split.sem, 1)

                ve.wait_ge(gates_used.sem, gates_used.by(l, N_GROUPS))
                ve.wait_ge(weight_made.sem, weight_made.by(l, BLOCKS - EARLY))
                for s in range(4):
                    split_weights(s, s)
                in_slots = (K * T + 2 * K * COLS) // T
                with ve.Fori(1, in_slots // 4) as i:
                    for s in range(4):
                        split_weights(4 * i + s, s)
                ve.wait_ge(w_split.sem, w_split.by(l, in_slots))
                V.memset(small[:, 0:1], 0.0).then_inc(slots_free.sem, 1)
                with ve.Fori(in_slots // 4, SHIFT_PRODUCTS[0] // 4) as i:
                    for s in range(4):
                        split_weights(4 * i + s, s)
                for n in range(SHIFT_PRODUCTS[0], SHIFT_PRODUCTS[-1] + K):
                    split_weights(n, n % 4)
                    if n in SHIFT_PRODUCTS:
                        m = SHIFT_PRODUCTS.index(n)
                        product = ada_product(l + 1, m, m % 2)
                    next(product)
                with ve.Fori((SHIFT_PRODUCTS[-1] + K) // 4, ROWS_AT // 4) as i:
                    for s in range(4):
                        split_weights(4 * i + s, s)
                for n in range(N_SHIFT):
                    modulation(l + 1, n, bank[4 + n], (l + 1) % L)
                diagonals(1)
                with ve.Fori(ROWS_AT // 4, BLOCKS // 4) as i:
                    for s in range(4):
                        split_weights(4 * i + s, s)

                ve.wait_ge(row_kept.sem, row_kept.by(l, 4))
                ve.wait_ge(y_added.sem, y_added.by(l, BLOCKS))
                for b in range(TB):
                    for n in range(2):
                        q = 2 * b + n
                        cols = slice(n * COLS, (n + 1) * COLS)
                        gated = tmp[:, (q % 2) * COLS:(q % 2 + 1) * COLS]
                        link(V.tensor_tensor(gated, y_bank[q][:, :], gate_row[:, cols], ALU.mult))
                        V.tensor_tensor(x_sb[:, b, cols], x_sb[:, b, cols], gated, ALU.add).then_inc(x_done.sem, 1)
                ve.wait_ge(x_done.sem, x_done.by(l, 4))
                V.memset(small[:, 0:1], 0.0).then_inc(arena_free.sem, 1)

        @block.tensor
        def _(pe):
            M = nc.tensor
            pe.wait_ge(masks_made.sem, 2)
            pe.wait_ge(c_in.sem, 16)
            M.transpose(bank[1][:, 0:K], c_rows, ident[0:K, 0:K]).then_inc(setup_transposed.sem, 1)
            pe.wait_ge(masks_made.sem, MASKS)
            pe.wait_ge(inputs_in.sem, 16 * 13)
            M.transpose(bank[0][:, 0:P], par_rows, ident[:, :]).then_inc(setup_transposed.sem, 1)
            M.matmul(bank[2][:, 0:L * ROWC], ones[0:1, :], row_consts, start=True, stop=True)\
                .then_inc(setup_transposed.sem, 1)
            pe.wait_ge(setup_done.sem, SETUP)
            pe.wait_ge(c_made.sem, 1)
            pe.nop().then_inc(arena_free.sem, 1)

            def modulate(l, n, s, to):
                pe.wait_ge(ada_summed.sem, ada_summed.by(l, n + 1))
                for j in range(COLS // P):
                    ins = M.matmul(to[:, j:j + 1], ada_sum[:, s, j * P:(j + 1) * P], ones[:, 0:1],
                                   start=True, stop=True)
                ins.then_inc(mod_summed.sem, 1)

            for n in range(N_SHIFT):
                modulate(0, n, n % 2, bank[4 + n])

            with pe.Fori(0, L) as l:
                def norm(which):
                    for b in range(TB):
                        pe.wait_ge(normed.sem, normed.by(l, TB * which + b + 1))
                        for k in range(K):
                            ins = M.transpose(bank[4 + 2 * b + k // 4][:, k % 4 * P:(k % 4 + 1) * P],
                                              x_norm[:, b, k * P:(k + 1) * P], ident[:, :])
                            if k % 4 == 3:
                                ins.then_inc(norm_transposed.sem, 1)

                norm(0)
                for made in h_t_made:
                    pe.wait_ge(made.sem, made.by(l, K))
                pe.wait_ge(forget_w_in.sem, forget_w_in.by(l, 16))
                for b in range(TB):
                    for k in range(K):
                        ins = M.matmul(bank[4][:, b * H:(b + 1) * H], h_t[:, k, b * P:(b + 1) * P], forget_w[:, k],
                                       start=k == 0, stop=k == K - 1)
                ins.then_inc(forget_summed.sem, 1)

                def chunk_products(n, pieces, before=lambda piece: None, input_of=None):
                    ins = None
                    for q in range(4):
                        if input_of is not None:
                            pe.wait_ge(h_lo_made.sem, h_lo_made.by(l, 4 * input_of + q + 1))
                        pe.wait_ge(part_hi.sem, part_hi.by(l, 4 * n + q + 1))
                        for low in (False, True):
                            if low:
                                pe.wait_ge(part_lo.sem, part_lo.by(l, 4 * n + q + 1))
                            for piece in range(len(pieces)):
                                if q == 0 and not low:
                                    before(piece)
                                for k in (2 * q, 2 * q + 1):
                                    at = slice(k % 2 * COLS, (k % 2 + 1) * COLS)
                                    weights = (rows_lo if low else rows_hi)[:, q % 2, at]
                                    ins = pieces[piece](k, weights, low) or ins
                        ins.then_inc(parts_used.sem, 1)

                def tokens_first(to, b, first=0, last=K - 1):
                    def make(k, weights, low):
                        if not first <= k <= last:
                            return None
                        hi, lo = (h[:, k, b * P:(b + 1) * P] for h in (h_hi, h_lo))
                        ins = M.matmul(to[:, :], hi, weights, start=k == first and not low, stop=k == last and low)
                        if not low:
                            ins = M.matmul(to[:, :], lo, weights, start=False, stop=False)
                        return ins
                    return make

                def project(n, s):
                    def ready(b):
                        if not isinstance(n, int):
                            pe.wait_ge(proj_kept.sem, proj_kept.by(l, 2 * (n - 2) + b + 1))
                    chunk_products(n, [tokens_first(bank[2 * s + b], b) for b in range(TB)], ready,
                                   0 if isinstance(n, int) and n == 0 else None)

                project(0, 0)
                project(1, 1)
                with pe.Fori(1, N_PROJ // 2) as i:
                    for s in range(2):
                        n = 2 * i + s
                        project(n, s)
                        pe.wait_ge(mod_made.sem, mod_made.by(l, n + 1))
                        modulate(l, n + 2, s, bank[6 + s])

                pe.wait_ge(log_f_made.sem, log_f_made.by(l, 1))
                M.matmul(bank[5][:, 0:H], cumsum_tri[:, :], small[:, 0:H], start=True, stop=True)
                M.matmul(bank[5][:, H:2 * H], cumsum_tri[:, :], small[:, H:2 * H], start=True, stop=False)
                M.matmul(bank[5][:, H:2 * H], ones[:, :], small[:, 0:H], start=False, stop=True)\
                    .then_inc(cum_f_summed.sem, 1)
                pe.wait_ge(aug_made.sem, aug_made.by(l, 1))
                pe.wait_ge(proj_kept.sem, proj_kept.by(l, TB * N_PROJ))
                pe.wait_ge(mod_made.sem, mod_made.by(l, N_ADA))

                def turn_qk(n):
                    if n >= 2:
                        pe.wait_ge(qk_kept.sem, qk_kept.by(l, n - 1))
                    for which in range(2):
                        for b in range(TB):
                            cols = slice((2 * which + b) * P, (2 * which + b + 1) * P)
                            if n < H:
                                ins = M.transpose(bank[4 + n % 2][0:AUG, cols], aug[:, which, b, n], ident[:, :])
                            else:
                                at = (3 + which) * COLS + (n - H) * P
                                ins = M.transpose(bank[4 + n % 2][:, cols], proj[:, b, at:at + P], ident[:, :])
                    ins.then_inc(qk_turned.sem, 1)

                def fox_scores(h):
                    pe.wait_ge(qk_kept.sem, qk_kept.by(l, h + 1))
                    if h >= 2:
                        pe.wait_ge(fox_exp.sem, fox_exp.by(l, 2 * (h - 1)))
                    q, k = fox_qk[0:AUG, h, 0:T], fox_qk[0:AUG, h, T:2 * T]
                    to = bank[h % 2]
                    M.matmul(to[:, 0:CAUSAL], ident_r[:, :], fox_mask[:, :], start=True, stop=False)
                    M.matmul(to[:, 0:P], q[:, 0:P], k[:, 0:P], start=False, stop=False)
                    M.matmul(to[:, P:CAUSAL], q[:, P:T], k[:, 0:T], start=False, stop=True)\
                        .then_inc(fox_scored.sem, 1)

                def turn_probs(h):
                    pe.wait_ge(fox_probs.sem, fox_probs.by(l, h + 1))
                    if h >= 2:
                        pe.wait_ge(probs_kept.sem, probs_kept.by(l, h - 1))
                    for n in range(3):
                        ins = M.transpose(bank[2 + h % 2][:, n * P:(n + 1) * P],
                                          probs[:, h % 2, n * P:(n + 1) * P], ident[:, :])
                    ins.then_inc(probs_turned.sem, 1)

                def values(h, group):
                    n = group * H // 2 + h // 2
                    if n >= 2 and h % 2 == 0:
                        pe.wait_ge(y_split.sem, y_split.by(l, n - 1))
                    to = bank[6 + n % 2][h % 2 * HD:(h % 2 + 1) * HD, :]
                    at = (2 + 3 * group) * COLS + h * HD
                    M.matmul(to[:, 0:T], proj[:, 0, at:at + HD], probs_t[:, h % 2, 0:T], start=True, stop=False)
                    ins = M.matmul(to[:, P:T], proj[:, 1, at:at + HD], probs_t[:, h % 2, T:CAUSAL],
                                   start=False, stop=True)
                    if h % 2:
                        ins.then_inc(y_summed.sem, 1)

                turn_qk(0)
                turn_qk(1)
                for h in range(H + 3):
                    if h < H:
                        fox_scores(h)
                        turn_qk(h + 2)
                    if h >= 3:
                        pe.wait_ge(probs_kept.sem, probs_kept.by(l, h - 2))
                        values(h - 3, 0)
                    if 2 <= h < H + 2:
                        turn_probs(h - 2)
                turn_qk(H + 2)
                turn_qk(H + 3)

                def sb_scores(h, to, stop):
                    half = slice(h % 2 * HD, (h % 2 + 1) * HD)
                    q, k = sb_qk[half, h // 2, 0:T], sb_qk[half, h // 2, T:2 * T]
                    M.matmul(to[:, 0:CAUSAL], ident_r[:, :], sb_mask[:, :], start=True, stop=False)
                    M.matmul(to[:, 0:T], k[:, 0:P], q, start=False, stop=False)
                    return M.matmul(to[:, T:CAUSAL], k[:, P:T], q[:, P:T], start=False, stop=stop)

                def sb_z(h):
                    pe.wait_ge(qk_kept.sem, qk_kept.by(l, H + (H // 2 if h == 2 else h // 2 + 1)))
                    if h >= 4:
                        pe.wait_ge(sb_keep_made.sem, sb_keep_made.by(l, h - 3))
                    sb_scores(h, z_bank[h % 4], True).then_inc(sb_scored.sem, 1)

                def sb_logits(h):
                    keep = log_keep[:, h % 2]
                    to = bank[2 + h % 2]
                    if h >= 2:
                        pe.wait_ge(sb_weights.sem, sb_weights.by(l, h - 1))
                    sb_scores(h, to, False)
                    pe.wait_ge(sb_keep_made.sem, sb_keep_made.by(l, h + 1))
                    M.matmul(to[:, 0:T], neg_suffix_tri[:, :], keep[:, 0:T], start=False, stop=False)
                    M.matmul(to[:, P:T], neg_ones[:, :], keep[:, T:CAUSAL], start=False, stop=False)
                    M.matmul(to[:, T:CAUSAL], neg_suffix_tri[:, :], keep[:, T:CAUSAL], start=False, stop=True)\
                        .then_inc(sb_summed.sem, 1)

                sb_z(0)
                sb_z(1)
                for h in range(H + 1):
                    if h + 2 < H:
                        sb_z(h + 2)
                    if h < H:
                        sb_logits(h)
                    if h >= 1:
                        pe.wait_ge(sb_weights.sem, sb_weights.by(l, h))
                        values(h - 1, 1)

                pe.wait_ge(y_split.sem, y_split.by(l, H))
                for n in range(2):
                    chunk_products(AT_BRANCH + n, [tokens_first(bank[4 * n + 2 * b + g], b, 4 * g, 4 * g + 3)
                                                   for g in range(2) for b in range(TB)])

                for n in range(4):
                    b, half = n // 2, n % 2
                    if half == 0:
                        pe.wait_ge(merged_made.sem, merged_made.by(l, 3 + b))
                    for j in range(4):
                        k = 4 * half + j
                        ins = M.transpose(bank[4 + n][:, j * P:(j + 1) * P], merged[:, b, k * P:(k + 1) * P],
                                          ident[:, :])
                    ins.then_inc(merged_turned.sem, 1)

                def gate_rows(which):
                    pe.wait_ge(diag_made.sem, diag_made.by(l, which + 1))
                    for k in range(K):
                        to = bank[(0 if which == 0 else 4) + k // 4]
                        ins = M.matmul(to[:, k % 4 * P:(k % 4 + 1) * P], ones[:, :], diag[:, k],
                                       start=True, stop=True)
                        if k % 4 == 3:
                            ins.then_inc(row_summed.sem, 1)

                pe.wait_ge(merged_split.sem, merged_split.by(l, 4))
                chunk_products(AT_OUT, [tokens_first(bank[2 + b], b) for b in range(TB)])
                gate_rows(0)
                chunk_products(AT_OUT + 1, [tokens_first(bank[4 + b], b) for b in range(TB)])

                norm(1)

                def head_queries(h):
                    def make(k, weights, low):
                        w = weights[:, h % 4 * P:(h % 4 + 1) * P]
                        ins = M.matmul(bank[h][:, 0:T], w, h_hi[:, k], start=k == 0 and not low,
                                       stop=k == K - 1 and low)
                        if not low:
                            ins = M.matmul(bank[h][:, 0:T], w, h_lo[:, k], start=False, stop=False)
                        return ins
                    return make

                for n in range(2):
                    chunk_products(AT_WQ + n, [head_queries(4 * n + h) for h in range(4)],
                                   input_of=1 if n == 0 else None)
                pe.wait_ge(keys_in.sem, keys_in.by(l, 32))
                pe.wait_ge(pq_kept.sem, pq_kept.by(l, 4))
                for h in range(H):
                    ins = M.transpose(bank[2 + h // 4][:, h % 4 * P:(h % 4 + 1) * P], keys[:, h], ident[:, :])
                    if h % 4 == 3:
                        ins.then_inc(keys_turned.sem, 1)
                pe.wait_ge(keys_kept.sem, keys_kept.by(l, 2))
                pe.wait_ge(pq_kept.sem, pq_kept.by(l, H))
                for b in range(TB):
                    for n in range(4):
                        w, g = n % 2, n // 2
                        half = slice(w * HD, (w + 1) * HD)
                        for j in range(4):
                            h = 4 * g + j
                            ins = M.matmul(bank[(4 if b == 0 else 0) + 2 * w + g][:, j * P:(j + 1) * P],
                                           pq_t[half, h, b * P:(b + 1) * P], keys_t[half, h],
                                           start=True, stop=True)
                        ins.then_inc(scored.sem, 1)

                def turn_u(n, s, i, first=False):
                    pe.wait_ge(u_landed[s].sem, u_landed[s].by(l, 16 * i + 16))
                    for half in range(2):
                        if not first:
                            pe.wait_ge(ut_lo_made.sem, ut_lo_made.by(l, 2 * (n - 1) + half + 1))
                        for j in range(4):
                            k = 4 * half + j
                            ins = M.transpose(ut_bank[half][:, j * P:(j + 1) * P],
                                              rows_in[:, s, k * P:(k + 1) * P], ident[:, :])
                        ins.then_inc(ut_turned.sem, 1)

                def inputs_sum(n, s, wait=True):
                    pe.wait_ge(ut_lo_made.sem, ut_lo_made.by(l, 2 * n + 2))
                    if wait:
                        pe.wait_ge(act_made.sem, act_made.by(l, n - 1))
                    for k in range(K):
                        hi, lo = rows_hi[:, s, k * P:(k + 1) * P], rows_lo[:, s, k * P:(k + 1) * P]
                        to = act_bank[s][:, 0:T]
                        M.matmul(to, hi, h_hi[:, k], start=k == 0, stop=False)
                        M.matmul(to, hi, h_lo[:, k], start=False, stop=False)
                        ins = M.matmul(to, lo, h_hi[:, k], start=False, stop=k == K - 1)
                    ins.then_inc(act_summed.sem, 1)

                pe.wait_ge(scores_kept.sem, scores_kept.by(l, 3))
                pe.wait_ge(last_scores_kept.sem, last_scores_kept.by(l, 1))
                turn_u(0, 0, 0, first=True)
                turn_u(1, 1, 0)
                inputs_sum(0, 0, wait=False)
                turn_u(2, 0, 1)
                inputs_sum(1, 1, wait=False)

                def early_blocks(first, after):
                    with pe.Fori(first // 2, after // 2) as i:
                        turn_u(2 * i + 1, 1, i)
                        inputs_sum(2 * i, 0)
                        turn_u(2 * i + 2, 0, i + 1)
                        inputs_sum(2 * i + 1, 1)

                early_blocks(2, ROUTED)
                pe.wait_ge(scores_kept.sem, scores_kept.by(l, 3 * TB))
                pe.wait_ge(route_made.sem, route_made.by(l, 1))
                for b in range(TB):
                    for w in range(3):
                        ins = M.transpose(bank[b][:, w * P:(w + 1) * P], routed[:, b, w], ident[:, :])
                    ins.then_inc(route_turned.sem, 1)
                early_blocks(ROUTED, EARLY)

                def token_gates(g, j, first=False):
                    pe.wait_ge(hot2_made.sem, hot2_made.by(l, g + 1))
                    pe.wait_ge(hot1_gated.sem, hot1_gated.by(l, g + 1))
                    if not first:
                        pe.wait_ge(gates_used.sem, gates_used.by(l, g - 3))
                    for t in range(GROUP):
                        at = j % 2 * GROUP + t
                        ins = M.matmul(gate_bank[j][:, t * P:(t + 1) * P], hot2[:, at], hot1[:, at],
                                       start=True, stop=True)
                    ins.then_inc(gates_summed.sem, 1)

                def gates_and_block(i, m, first=False):
                    n = EARLY + 2 * i + m
                    for j in (2 * m, 2 * m + 1):
                        token_gates(4 * i + j, j, first)
                    turn_u(n + 1, 1 - m, EARLY // 2 + i + m)
                    inputs_sum(n, m)

                pe.wait_ge(route_kept.sem, route_kept.by(l, TB))
                pe.wait_ge(last_scores_kept.sem, last_scores_kept.by(l, TB))
                for m in range(2):
                    gates_and_block(0, m, first=True)
                with pe.Fori(1, MIDDLE // 2) as i:
                    for m in range(2):
                        gates_and_block(i, m)
                turn_u(LATE_AT + 1, 1, LATE_AT // 2)
                with pe.Fori(LATE_AT // 2, BLOCKS // 2 - 1) as i:
                    for s in range(2):
                        inputs_sum(2 * i + s, s)
                        turn_u(2 * i + s + 2, s, i + 1)
                inputs_sum(BLOCKS - 2, 0)
                inputs_sum(BLOCKS - 1, 1)

                def outputs_add(n, s, start=False, stop=False):
                    pe.wait_ge(w_split.sem, w_split.by(l, n + 1))
                    pe.wait_ge(v_hi_made.sem, v_hi_made.by(l, n + 1))
                    for part_no, (w, v) in enumerate(((w_hi, rows_hi), (w_lo, rows_hi), (w_hi, rows_lo))):
                        if part_no == 2:
                            pe.wait_ge(v_split.sem, v_split.by(l, n + 1))
                        for b in range(TB):
                            for half in range(2):
                                ins = M.matmul(y_bank[2 * b + half][:, :], w[:, s, b * P:(b + 1) * P],
                                               v[:, s, half * COLS:(half + 1) * COLS],
                                               start=start and part_no == 0, stop=stop and part_no == 2)
                    ins.then_inc(y_added.sem, 1)

                pe.wait_ge(gates_used.sem, gates_used.by(l, N_GROUPS))
                outputs_add(0, 0, start=True)
                outputs_add(1, 1)
                lag = 10
                with pe.Fori(1, (SHIFT_PRODUCTS[0] + lag) // 2) as i:
                    for s in range(2):
                        outputs_add(2 * i + s, s)
                for n in range(SHIFT_PRODUCTS[0] + lag, SHIFT_PRODUCTS[-1] + lag + 2):
                    if n - lag in SHIFT_PRODUCTS:
                        m = SHIFT_PRODUCTS.index(n - lag)
                        modulate(l + 1, m, m % 2, bank[4 + m])
                    outputs_add(n, n % 2)
                rows_at = ROWS_AT + 4
                with pe.Fori((SHIFT_PRODUCTS[-1] + lag) // 2 + 1, rows_at // 2) as i:
                    for s in range(2):
                        outputs_add(2 * i + s, s)
                pe.wait_ge(mod_made.sem, mod_made.by(l + 1, N_SHIFT))
                gate_rows(1)
                with pe.Fori(rows_at // 2, BLOCKS // 2 - 1) as i:
                    for s in range(2):
                        outputs_add(2 * i + s, s)
                outputs_add(BLOCKS - 2, 0)
                outputs_add(BLOCKS - 1, 1, stop=True)


_INS = ['x', 'c', 'ada_w', 'ada_b', 'attn_norm', 'ffn_norm', 'w_in', 'fox_bf', 'fox_q_gain', 'fox_k_gain',
        'w_branch', 'w_out', 'peer_wq', 'peer_k1', 'peer_k2', 'peer_u', 'peer_v']


def kernel(**inputs):
    import numpy as np
    import concourse.bacc as bacc
    from concourse.bass_utils import run_bass_kernel_spmd

    nc = bacc.Bacc("TRN2", target_bir_lowering=False, num_devices=1)
    arrays, args = {}, []
    for name in _INS:
        a = np.ascontiguousarray(inputs[name])
        arrays[f"in_{name}"] = a
        args.append(nc.dram_tensor(f"in_{name}", a.shape, mybir.dt.from_np(a.dtype), kind="ExternalInput").ap())
    out = nc.dram_tensor("out", (1, T, D), F32, kind="ExternalOutput").ap()
    hybrid_fox_stickbreak_peer(nc, *args, out)
    r = run_bass_kernel_spmd(nc, [arrays], core_ids=[0])
    return r.results[0]["out"]
```
